# Optimizing a Trainium2 kernel written in Bass

```python
import math
import jax, jax.numpy as jnp
from jax import lax
import numpy as np

D_MODEL = 1024
BATCH = 1
SEQ = 512
DEPTH = 1
DEC_BATCH = 8
DEC_SEQ = 8
PAST_LEN = 4096
PAGE_SIZE = 128

CHUNK = 128
A_GROUPS = 4
A_WIDTH = 1024
A_GDIM = A_WIDTH // A_GROUPS
DN_HEADS = 8
DN_KDIM = 128
DN_VDIM = 128
DN_QK = DN_HEADS * DN_KDIM
DN_V = DN_HEADS * DN_VDIM
DN_CONV_CH = 2 * DN_QK + DN_V
CONV_W = 4
DN_CHUNK = 64
N_GROUPS = 4
EXP_PER_GROUP = 8
N_EXPERTS = N_GROUPS * EXP_PER_GROUP
TOP_K = 2
D_EXPERT = 256
N_MOD = 6
EPS = 1e-6
IN_SIZES = (A_WIDTH, A_WIDTH, DN_CONV_CH, DN_V, DN_HEADS, DN_HEADS, D_MODEL, D_MODEL)
IN_WIDTH = A_WIDTH * 2 + DN_CONV_CH + DN_V + DN_HEADS * 2 + D_MODEL * 2

kernel_name = 'hybrid_gmlp_gdn_hmoe_step'

def rmsnorm(x, w):
    xf = x.astype(jnp.float32)
    y = xf * lax.rsqrt(jnp.mean(xf * xf, axis=-1, keepdims=True) + EPS)
    return (y * w.astype(jnp.float32)).astype(x.dtype)

def layernorm(x, w, b):
    xf = x.astype(jnp.float32)
    mu = jnp.mean(xf, axis=-1, keepdims=True)
    xc = xf - mu
    var = jnp.mean(xc * xc, axis=-1, keepdims=True)
    return (xc * lax.rsqrt(var + EPS) * w.astype(jnp.float32) + b.astype(jnp.float32)).astype(x.dtype)

def l2norm(x):
    xf = x.astype(jnp.float32)
    return xf * lax.rsqrt(jnp.sum(xf * xf, axis=-1, keepdims=True) + EPS)

def causal_conv(x, buf, w):
    T = x.shape[1]
    xp = jnp.concatenate([buf.astype(x.dtype), x], axis=1)
    y = xp[:, 0:T] * w[0]
    for j in range(1, CONV_W):
        y = y + xp[:, j:j + T] * w[j]
    return y, xp[:, -(CONV_W - 1):]

def gated_delta_rule(q, k, v, g, beta, s0, chunk):
    B, T, H, K = q.shape
    V = v.shape[-1]
    N = T // chunk
    f32 = jnp.float32

    def chunks(a):
        return jnp.swapaxes(a.reshape((B, N, chunk) + a.shape[2:]), 2, 3)

    qc = chunks(q.astype(f32) * (K ** -0.5))
    kc = chunks(k.astype(f32))
    vc = chunks(v.astype(f32))
    gc = jnp.cumsum(chunks(g.astype(f32)), axis=-1)
    bc = chunks(beta.astype(f32))
    tril = jnp.tril(jnp.ones((chunk, chunk), dtype=bool))
    strict = jnp.tril(jnp.ones((chunk, chunk), dtype=bool), -1)
    diff = gc[..., :, None] - gc[..., None, :]
    decay = jnp.where(tril, jnp.exp(jnp.minimum(diff, 0.0)), 0.0)
    kb = kc * bc[..., None]
    vb = vc * bc[..., None]
    lmat = jnp.where(strict, jnp.einsum('bnhck,bnhsk->bnhcs', kb, kc) * decay, 0.0)
    rhs = jnp.concatenate([vb, kb * jnp.exp(gc)[..., None]], axis=-1)
    sol = lax.linalg.triangular_solve(lmat, rhs, left_side=True, lower=True, unit_diagonal=True)
    uc, wc = sol[..., :V], sol[..., V:]
    attn = jnp.where(tril, jnp.einsum('bnhck,bnhsk->bnhcs', qc, kc) * decay, 0.0)

    def step(S, xs):
        q_i, k_i, u_i, w_i, a_i, g_i = xs
        v_new = u_i - jnp.einsum('bhck,bhkv->bhcv', w_i, S)
        o = jnp.einsum('bhck,bhkv->bhcv', q_i * jnp.exp(g_i)[..., None], S) + jnp.einsum('bhcs,bhsv->bhcv', a_i, v_new)
        g_last = g_i[..., -1]
        S = S * jnp.exp(g_last)[..., None, None] + jnp.einsum(
            'bhck,bhcv->bhkv', k_i * jnp.exp(g_last[..., None] - g_i)[..., None], v_new)
        return S, o

    xs = tuple(jnp.moveaxis(a, 1, 0) for a in (qc, kc, uc, wc, attn, gc))
    S, o = lax.scan(step, s0.astype(f32), xs)
    o = jnp.transpose(o, (1, 0, 3, 2, 4)).reshape(B, T, H, V)
    return o, S

def token_mixers(h, conv_buf, s0, w_in, conv_w, a_log, dt_bias, dn_norm, ln_v_w, ln_v_b, w_s, b_s, w_pa, w_pb, w_o):
    B, T, _ = h.shape
    z = h @ w_in
    zu, zv, zqkv, zz, zb, za, ga, gb = jnp.split(z, np.cumsum(IN_SIZES)[:-1].tolist(), axis=-1)
    zu = jax.nn.gelu(zu, approximate=False)
    vn = layernorm(jax.nn.gelu(zv, approximate=False), ln_v_w, ln_v_b)
    L = min(CHUNK, T)
    N = T // L
    wm = (w_s * jnp.tril(jnp.ones((CHUNK, CHUNK), w_s.dtype)))[:, :L, :L]
    sv = jnp.einsum('gts,bnsgc->bntgc', wm, vn.reshape(B, N, L, A_GROUPS, A_GDIM))
    sv = sv + jnp.transpose(b_s[:, :L])[None, None, :, :, None]
    a_out = zu * sv.reshape(B, T, A_WIDTH)
    qkv, conv_new = causal_conv(zqkv, conv_buf, conv_w)
    qkv = jax.nn.silu(qkv)
    q, k, v = jnp.split(qkv, [DN_QK, 2 * DN_QK], axis=-1)
    q = l2norm(q.reshape(B, T, DN_HEADS, DN_KDIM))
    k = l2norm(k.reshape(B, T, DN_HEADS, DN_KDIM))
    v = v.reshape(B, T, DN_HEADS, DN_VDIM)
    beta = jax.nn.sigmoid(zb.astype(jnp.float32))
    g = -jnp.exp(a_log.astype(jnp.float32)) * jax.nn.softplus(za.astype(jnp.float32) + dt_bias.astype(jnp.float32))
    o, s_new = gated_delta_rule(q, k, v, g, beta, s0, min(DN_CHUNK, T))
    o = rmsnorm(o.astype(h.dtype), dn_norm) * jax.nn.silu(zz.reshape(B, T, DN_HEADS, DN_VDIM))
    b_out = o.reshape(B, T, DN_V)
    m = jax.nn.sigmoid(ga) * (a_out @ w_pa) + jax.nn.sigmoid(gb) * (b_out @ w_pb)
    return m @ w_o, conv_new, s_new.astype(h.dtype), vn

def hier_moe(h, w_rg, b_rg, w_re, b_re, w_e_gate, w_e_up, w_e_down):
    f32 = jnp.float32
    glog = (h @ w_rg).astype(f32) + b_rg.astype(f32)
    gprob = jax.nn.softmax(glog, axis=-1)
    gtop, gsel = lax.top_k(glog, 1)
    gp = jnp.take_along_axis(gprob, gsel, axis=-1)
    elog = ((h @ w_re).astype(f32) + b_re.astype(f32)).reshape(h.shape[:-1] + (N_GROUPS, EXP_PER_GROUP))
    elog_g = jnp.take_along_axis(elog, gsel[..., None], axis=-2)[..., 0, :]
    etop, esel = lax.top_k(elog_g, TOP_K)
    ew = jax.nn.softmax(etop, axis=-1) * gp
    exp_w = jnp.sum(jax.nn.one_hot(esel, EXP_PER_GROUP, dtype=f32) * ew[..., None], axis=-2)
    combine = jax.nn.one_hot(gsel[..., 0], N_GROUPS, dtype=f32)[..., :, None] * exp_w[..., None, :]
    combine = combine.astype(h.dtype)
    out = jnp.zeros_like(h)
    for gi in range(N_GROUPS):
        a = jnp.einsum('btd,edf->btef', h, w_e_gate[gi])
        u = jnp.einsum('btd,edf->btef', h, w_e_up[gi])
        act = jax.nn.silu(a) * u * combine[..., gi, :, None]
        out = out + jnp.einsum('btef,efd->btd', act, w_e_down[gi])
    return out

def decoder_layer(x, c, conv_buf, s0, w_ada, b_ada, norm1, norm2, w_in, conv_w, a_log, dt_bias, dn_norm,
                  ln_v_w, ln_v_b, w_s, b_s, w_pa, w_pb, w_o, w_rg, b_rg, w_re, b_re, w_e_gate, w_e_up, w_e_down):
    B = x.shape[0]
    mod = (jax.nn.silu(c) @ w_ada + b_ada).reshape(B, N_MOD, 1, D_MODEL)
    sh1, sc1, g1, sh2, sc2, g2 = [mod[:, i] for i in range(N_MOD)]
    h = rmsnorm(x, norm1) * (1 + sc1) + sh1
    mix, conv_new, s_new, vn = token_mixers(h, conv_buf, s0, w_in, conv_w, a_log, dt_bias, dn_norm,
                                            ln_v_w, ln_v_b, w_s, b_s, w_pa, w_pb, w_o)
    x = x + g1 * mix
    h = rmsnorm(x, norm2) * (1 + sc2) + sh2
    x = x + g2 * hier_moe(h, w_rg, b_rg, w_re, b_re, w_e_gate, w_e_up, w_e_down)
    return x, conv_new, s_new, vn

def setup_inputs(seed: int = 0) -> dict:
    key = jax.random.key(seed)
    ks = jax.random.split(key, 32)
    f32 = jnp.float32

    def nrm(k, shape, scale):
        return jax.random.normal(k, shape, f32) * scale

    inp = {}
    inp['x_prompt'] = nrm(ks[0], (BATCH, SEQ, D_MODEL), 1.0)
    inp['x_sample'] = nrm(ks[1], (DEC_BATCH, DEC_SEQ, D_MODEL), 1.0)
    inp['c_prompt'] = nrm(ks[2], (BATCH, D_MODEL), 1.0)
    inp['c_sample'] = nrm(ks[3], (DEC_BATCH, D_MODEL), 1.0)
    inp['state_conv'] = nrm(ks[4], (DEPTH, DEC_BATCH, CONV_W - 1, DN_CONV_CH), 1.0)
    inp['state_delta'] = nrm(ks[5], (DEPTH, DEC_BATCH, DN_HEADS, DN_KDIM, DN_VDIM), 0.05)
    inp['w_ada'] = nrm(ks[6], (DEPTH, D_MODEL, N_MOD * D_MODEL), 0.5 * D_MODEL ** -0.5)
    inp['b_ada'] = nrm(ks[7], (DEPTH, N_MOD * D_MODEL), 0.01)
    inp['norm1'] = 1.0 + nrm(ks[8], (DEPTH, D_MODEL), 0.02)
    inp['norm2'] = 1.0 + nrm(ks[9], (DEPTH, D_MODEL), 0.02)
    inp['w_in'] = nrm(ks[10], (DEPTH, D_MODEL, IN_WIDTH), D_MODEL ** -0.5)
    inp['conv_w'] = nrm(ks[11], (DEPTH, CONV_W, DN_CONV_CH), CONV_W ** -0.5)
    inp['a_log'] = jnp.log(jax.random.uniform(ks[12], (DEPTH, DN_HEADS), f32, 1.0, 16.0))
    dt = jnp.exp(jax.random.uniform(ks[13], (DEPTH, DN_HEADS), f32, math.log(1e-3), math.log(1e-1)))
    inp['dt_bias'] = dt + jnp.log(-jnp.expm1(-dt))
    inp['dn_norm'] = 1.0 + nrm(ks[14], (DEPTH, DN_VDIM), 0.02)
    inp['ln_v_w'] = 1.0 + nrm(ks[15], (DEPTH, A_WIDTH), 0.02)
    inp['ln_v_b'] = nrm(ks[16], (DEPTH, A_WIDTH), 0.02)
    inp['w_s'] = nrm(ks[17], (DEPTH, A_GROUPS, CHUNK, CHUNK), CHUNK ** -0.5)
    inp['b_s'] = 1.0 + nrm(ks[18], (DEPTH, A_GROUPS, CHUNK), 0.1)
    inp['w_pa'] = nrm(ks[19], (DEPTH, A_WIDTH, D_MODEL), A_WIDTH ** -0.5)
    inp['w_pb'] = nrm(ks[20], (DEPTH, DN_V, D_MODEL), DN_V ** -0.5)
    inp['w_o'] = nrm(ks[21], (DEPTH, D_MODEL, D_MODEL), D_MODEL ** -0.5)
    inp['w_rg'] = nrm(ks[22], (DEPTH, D_MODEL, N_GROUPS), D_MODEL ** -0.5)
    inp['b_rg'] = nrm(ks[23], (DEPTH, N_GROUPS), 0.01)
    inp['w_re'] = nrm(ks[24], (DEPTH, D_MODEL, N_EXPERTS), D_MODEL ** -0.5)
    inp['b_re'] = nrm(ks[25], (DEPTH, N_EXPERTS), 0.01)
    inp['w_e_gate'] = nrm(ks[26], (DEPTH, N_GROUPS, EXP_PER_GROUP, D_MODEL, D_EXPERT), D_MODEL ** -0.5)
    inp['w_e_up'] = nrm(ks[27], (DEPTH, N_GROUPS, EXP_PER_GROUP, D_MODEL, D_EXPERT), D_MODEL ** -0.5)
    inp['w_e_down'] = nrm(ks[28], (DEPTH, N_GROUPS, EXP_PER_GROUP, D_EXPERT, D_MODEL), D_EXPERT ** -0.5)
    inp['final_norm'] = 1.0 + nrm(ks[29], (D_MODEL,), 0.02)
    return inp

def reference(x_prompt, x_sample, c_prompt, c_sample, state_conv, state_delta, w_ada, b_ada, norm1, norm2,
              w_in, conv_w, a_log, dt_bias, dn_norm, ln_v_w, ln_v_b, w_s, b_s, w_pa, w_pb, w_o,
              w_rg, b_rg, w_re, b_re, w_e_gate, w_e_up, w_e_down, final_norm):
    xp, xs = x_prompt, x_sample
    bp = x_prompt.shape[0]
    zero_conv = jnp.zeros((bp, CONV_W - 1, DN_CONV_CH), x_prompt.dtype)
    zero_state = jnp.zeros((bp, DN_HEADS, DN_KDIM, DN_VDIM), x_prompt.dtype)
    conv_p, conv_s, delta_p, delta_s, vrows_s = [], [], [], [], []
    for l in range(DEPTH):
        lw = [p[l] for p in (w_ada, b_ada, norm1, norm2, w_in, conv_w, a_log, dt_bias, dn_norm, ln_v_w, ln_v_b,
                             w_s, b_s, w_pa, w_pb, w_o, w_rg, b_rg, w_re, b_re, w_e_gate, w_e_up, w_e_down)]
        xp, cp, sp, _ = decoder_layer(xp, c_prompt, zero_conv, zero_state, *lw)
        xs, cs, ss, vs = decoder_layer(xs, c_sample, state_conv[l], state_delta[l], *lw)
        conv_p.append(cp)
        conv_s.append(cs)
        delta_p.append(sp)
        delta_s.append(ss)
        vrows_s.append(vs)
    y_prompt = rmsnorm(xp, final_norm)
    y_sample = rmsnorm(xs, final_norm)
    conv_prompt = jnp.stack(conv_p)
    conv_sample = jnp.stack(conv_s)
    delta_prompt = jnp.stack(delta_p)
    delta_sample = jnp.stack(delta_s)
    chunk_v_sample = jnp.stack(vrows_s)
    return (y_prompt, y_sample, conv_prompt, conv_sample, delta_prompt, delta_sample, chunk_v_sample)


_drawn_inputs = setup_inputs


def setup_inputs(seed=0):
    import zlib

    import numpy as np

    out = dict(_drawn_inputs(seed))
    spreads = {}
    factors = {'b_ada': 2.874,
     'norm2': 4.679,
     'dn_norm': 8.0,
     'ln_v_w': 8.087,
     'ln_v_b': 8.126,
     'b_s': 4.455,
     'b_rg': 8.0,
     'b_re': 7.703,
     'final_norm': 8.194}
    for name, (base, spread) in spreads.items():
        noise = np.random.default_rng([zlib.crc32(name.encode()), seed]).standard_normal(out[name].shape)
        drawn = base * np.exp(spread * noise) if base else spread * noise
        out[name] = __import__('jax').numpy.asarray(drawn.astype(out[name].dtype))
    for name, factor in factors.items():
        out[name] = (out[name] * factor).astype(out[name].dtype)
    return out
```

```python
import numpy as np
import concourse.bass as bass
from concourse import mybir
from contextlib import ExitStack, contextmanager

F32 = mybir.dt.float32
BF16 = mybir.dt.bfloat16
I32 = mybir.dt.int32
U32 = mybir.dt.uint32
U16 = mybir.dt.uint16
ALU = mybir.AluOpType
ACT = mybir.ActivationFunctionType
AX = mybir.AxisListType

D = 1024
KC = D // 128
SEQ = 512
NB, NS = 8, 8
TOK = SEQ + NB * NS
HALF = TOK // 2
NT = 5
ROWS = [128] * 4 + [NB * NS]
H = 8
EPS = 1e-6
NG, NE, KTOP, DE = 4, 32, 2, 256
GW = 512
NCH = 24
HIST = 3
PST = HIST + SEQ
SST = HIST + NS


def tile_cols(t):
    return slice(128 * t, 128 * t + ROWS[t])


class Stream:

    def __init__(self, nc, ctx, ins):
        self.ring = ctx.enter_context(nc.sbuf_tensor("w_ring", [128, 2, KC, GW], F32))
        self.arrived = [ctx.enter_context(nc.semaphore(f"w_arrived{i}")) for i in range(2)]
        w_in, w_ada = ins["w_in"][0], ins["w_ada"][0]
        self.src, self.at = [], {}

        def add(name, w, col, width=GW):
            self.at[name] = len(self.src)
            self.src.append((w[:, col:col + width].rearrange("(c p) n -> p c n", p=128), width))

        for j in range(12):
            add(f"ada{j}", w_ada, GW * j)
        for name, col, n in (("zv", 1024, 2), ("zu", 0, 2), ("qkv", 2048, 6)):
            for j in range(n):
                add(f"{name}{j}", w_in, col + GW * j)
        add("ba", w_in, 6144, 16)
        for j in range(2):
            add(f"zz{j}", w_in, 5120 + GW * j)
        for gate, col, w in (("ga", 6160, ins["w_pa"][0]), ("gb", 7184, ins["w_pb"][0])):
            for j in range(2):
                add(f"{gate}{j}", w_in, col + GW * j)
                add(f"{gate}p{j}", w, GW * j)
        for j in range(2):
            add(f"o{j}", ins["w_o"][0], GW * j)

    def load(self, sp, n, free=None):
        if n >= len(self.src):
            return
        if free is not None:
            sp.wait_ge(*free)
        src, width = self.src[n]
        sp.dma_start(self.ring[:, n % 2, :, 0:width], src).then_inc(self.arrived[n % 2], 16)

    def wait(self, pe, n):
        pe.wait_ge(self.arrived[n % 2], 16 * (n // 2 + 1))
        return self.ring[:, n % 2]


class Mem:
    pass


@contextmanager
def semaphores(nc):
    mine = []

    def sem(name):
        mine.append(nc.alloc_semaphore(name=name))
        return mine[-1]
    yield sem
    nc.all_engine_barrier()
    nc.clear_and_free_semaphores(mine)
    nc.all_engine_barrier()


def constants(nc, ctx, m):
    sb = lambda name, shape, dt=F32: ctx.enter_context(nc.sbuf_tensor(name, shape, dt))
    m.ident = sb("ident", [128, 128])
    m.ones = sb("ones", [128, 1])
    m.cum = [sb("cum_prompt", [128, 128]), sb("cum_new", [64, 64])]
    m.low = [sb("low_prompt", [128, 128]), sb("low_new", [64, 64])]
    m.blk = [sb("blk_prompt", [128, 128]), sb("blk_new", [64, 64])]
    m.level = sb("level", [128, 7, 128], BF16)
    m.half = sb("minus_half", [128, 80])
    return m


def build_constants(nc, m, step):
    g = nc.gpsimd

    def keep(ap, pattern, base, mult, op=ALU.is_ge, fill=0.0):
        step(g.affine_select(out=ap, in_=ap, compare_op=op, fill=fill, base=base, pattern=pattern,
                             channel_multiplier=mult))

    step(g.memset(m.ident[:, :], 0.0))
    keep(m.ident[:, :], [[-1, 128]], 0, 1, ALU.not_equal, 1.0)
    step(g.memset(m.ones[:, :], 1.0))
    step(g.memset(m.half[:, :], -0.5))
    for kind, (n, b) in enumerate(((128, 128), (64, NS))):
        for x in (m.cum[kind], m.low[kind], m.blk[kind]):
            step(g.memset(x[:, :], 1.0))
            v = x[:, :].rearrange("p (b s) -> p b s", s=b)
            keep(v, [[-b, n // b], [0, b]], 0, 1)
            keep(v, [[b, n // b], [0, b]], b - 1, -1)
        keep(m.cum[kind][:, :], [[1, n]], 0, -1)
        keep(m.low[kind][:, :], [[-1, n]], 0, 1)
    step(g.memset(m.level[:, :, :], 0.0))
    v = m.level[:, 0].rearrange("p (b s) -> p b s", s=2)[:, :, 0]
    keep(v, [[-2, 64]], -1, 1, ALU.not_equal, 1.0)
    for l in range(1, 7):
        s = 1 << l
        v = m.level[:, l].rearrange("p (b two s) -> p b two s", two=2, s=s)[:, :, 1, :]
        step(g.memset(v, 1.0))
        keep(v, [[-2 * s, 64 // s], [0, s]], 0, 1)
        keep(v, [[2 * s, 64 // s], [0, s]], s - 1, -1)


def phase_modulation(nc, m, ins, st, psum):
    with ExitStack() as ctx:
        sb = lambda name, shape, dt=F32: ctx.enter_context(nc.sbuf_tensor(name, shape, dt))
        sem = ctx.enter_context(semaphores(nc))
        c9 = sb("c9", [9, D])
        cT = sb("cT", [128, KC, 9])
        bada = sb("bada9", [9, 6 * D])
        mod9 = sb("mod9", [9, 6 * D])
        n1row = sb("n1row", [8, 128])
        prow = sb("prow", [97, 128])
        n1T = sb("n1T", [128, KC])
        scale1 = sb("scale1", [128, KC, 9])
        shift1 = sb("shift1", [128, KC, 9])
        xt = sb("xt", [128, NT, D])
        sq = sb("x_sq", [128, D])
        ss = sb("x_ss", [128, NT])
        rs = sb("x_rs", [128, NT])
        cloaded, xloaded, bloaded, ploaded = sem("c_loaded"), sem("x_loaded"), sem("bada_loaded"), sem("p_loaded")
        csilu, cps, cTdone = sem("c_silu"), sem("cT_psum"), sem("cT_done")
        adamm, adaev, modtr, pstage = sem("ada_mm"), sem("ada_ev"), sem("mod_tr"), sem("p_stage")
        s1, xsq, xrs, xsc, xtr, hdone, sc1done, modst = (sem("pT_done"), sem("x_squared"), sem("x_rstd"), sem("x_scaled"),
                                                  sem("x_tr"), sem("h_done"), sem("scale1_done"), sem("mod_stored"))
        dv = sem("dve_steps1")
        pools = sem("pool_steps")
        with nc.Block() as block:
            @block.gpsimd
            def _(pool):
                n = [0]

                def step(ins_):
                    n[0] += 1
                    ins_.then_inc(pools, 1)
                    pool.wait_ge(pools, n[0])
                step(nc.gpsimd.memset(ss[:, :], 1.0))
                step(nc.gpsimd.memset(xt[64:128, NT - 1, :], 0.0))
                build_constants(nc, m, step)

            @block.sync
            def _(sp):
                for n in range(14):
                    st.load(sp, n, (adamm, n - 1) if n >= 2 else None)

            @block.scalar
            def _(act):
                act.dma_start(c9[0:1, :], ins["c_prompt"]).then_inc(cloaded, 16)
                act.dma_start(c9[1:9, :], ins["c_sample"]).then_inc(cloaded, 16)
                act.dma_start(n1row[:, :], ins["norm1"][0].rearrange("(a p) -> a p", p=128)).then_inc(ploaded, 16)
                act.dma_start(prow[0:96, :], ins["conv_w"][0].rearrange("j (c p) -> (j c) p", p=128)).then_inc(ploaded, 16)
                act.dma_start(prow[96:97, :], ins["dn_norm"]).then_inc(ploaded, 16)
                act.dma_start(bada[:, :], ins["b_ada"][0].partition_broadcast(9)).then_inc(bloaded, 16)
                for t in range(4):
                    act.dma_start(xt[:, t, :], ins["x_prompt"][0, tile_cols(t), :]).then_inc(xloaded, 16)
                act.dma_start(xt[0:64, 4, :], ins["x_sample"].rearrange("b s d -> (b s) d")).then_inc(xloaded, 16)
                act.wait_ge(cloaded, 32)
                nc.scalar.activation(c9[:, :], c9[:, :], ACT.Silu).then_inc(csilu, 1)
                act.wait_ge(xloaded, 80)
                act.wait_ge(pools, 2)
                for t in range(NT):
                    if t:
                        act.wait_ge(xsq, t)
                    nc.scalar.activation(sq[0:ROWS[t], :], xt[0:ROWS[t], t, :], ACT.Square,
                                         accum_out=ss[0:ROWS[t], t:t + 1]).then_inc(xsq, 1)
                act.wait_ge(dv, 1)
                nc.scalar.activation(rs[:, :], ss[:, :], ACT.Sqrt).then_inc(xrs, 1)
                act.wait_ge(dv, 2)
                for t in range(NT):
                    nc.scalar.activation(xt[:, t, :], xt[:, t, :], ACT.Copy, scale=rs[:, t:t + 1]).then_inc(xsc, 1)
                act.wait_ge(adaev, 12)
                act.dma_start(m.mod_dram, mod9[:, :]).then_inc(modst, 16)
                act.wait_ge(modst, 16)

            @block.tensor
            def _(pe):
                pe.wait_ge(pools, 4)
                pe.wait_ge(csilu, 1)
                for c in range(KC):
                    last = nc.tensor.transpose(psum[:, 7, 9 * c:9 * c + 9], c9[:, 128 * c:128 * c + 128], m.ident[0:9, 0:9])
                last.then_inc(cps, 1)
                pe.wait_ge(ploaded, 48)
                nc.tensor.transpose(psum[:, 6, 0:97], prow[:, :], m.ident[0:97, 0:97])
                nc.tensor.transpose(psum[:, 6, 100:108], n1row[:, :], m.ident[0:8, 0:8]).then_inc(pstage, 1)
                pe.wait_ge(cTdone, 1)

                def ada(j):
                    w = st.wait(pe, j)
                    if j >= 2:
                        pe.wait_ge(adaev, j - 1)
                    for c in range(KC):
                        last = nc.tensor.matmul(psum[0:9, j % 2, :], cT[:, c, :], w[:, c, :], start=c == 0, stop=c == KC - 1)
                    last.then_inc(adamm, 1)
                for j in range(4):
                    ada(j)
                pe.wait_ge(adaev, 4)
                pe.wait_ge(s1, 1)
                for c in range(16):
                    last = nc.tensor.transpose(psum[:, 6, 9 * c:9 * c + 9], mod9[:, 128 * c:128 * c + 128], m.ident[0:9, 0:9])
                last.then_inc(modtr, 1)
                for t in range(NT):
                    pe.wait_ge(xsc, t + 1)
                    if t >= 2:
                        pe.wait_ge(hdone, t - 1)
                    for c in range(KC):
                        bank = 2 + 2 * (t % 2) + c // 4
                        last = nc.tensor.transpose(psum[:, bank, 128 * (c % 4):128 * (c % 4) + ROWS[t]],
                                                   xt[0:ROWS[t], t, 128 * c:128 * c + 128], m.ident[0:ROWS[t], 0:ROWS[t]])
                    last.then_inc(xtr, 1)
                for j in range(4, 12):
                    ada(j)

            @block.vector
            def _(dve):
                v = nc.vector
                dve.wait_ge(cps, 1)
                v.tensor_copy(cT[:, :, :].rearrange("p c r -> p (c r)"), psum[:, 7, 0:72]).then_inc(cTdone, 1)
                dve.wait_ge(pstage, 1)
                v.tensor_copy(m.convT[:, :], psum[:, 6, 0:97])
                v.tensor_copy(n1T[:, :], psum[:, 6, 100:108]).then_inc(s1, 1)
                dve.wait_ge(xsq, NT)
                v.tensor_scalar(ss[:, :], ss[:, :], 1.0 / D, EPS, ALU.mult, ALU.add).then_inc(dv, 1)
                dve.wait_ge(xrs, 1)
                v.reciprocal(rs[:, :], rs[:, :]).then_inc(dv, 1)
                dve.wait_ge(bloaded, 16)

                def add_bias(j):
                    dve.wait_ge(adamm, j + 1)
                    v.tensor_tensor(mod9[:, GW * j:GW * j + GW], psum[0:9, j % 2, :], bada[:, GW * j:GW * j + GW],
                                    ALU.add).then_inc(adaev, 1)
                for j in range(4):
                    add_bias(j)
                dve.wait_ge(modtr, 1)
                dve.wait_ge(s1, 1)
                v.tensor_copy(shift1[:, :, :].rearrange("p c r -> p (c r)"), psum[:, 6, 0:72])
                v.tensor_scalar(scale1[:, :, :].rearrange("p c r -> p (c r)"), psum[:, 6, 72:144], 1.0, None, ALU.add).then_inc(dv, 1)
                dve.wait_ge(dv, 3)
                v.tensor_tensor(scale1[:, :, :], scale1[:, :, :], n1T[:, :].unsqueeze(2).broadcast_to([128, KC, 9]),
                                ALU.mult).then_inc(sc1done, 1)
                dve.wait_ge(sc1done, 1)
                for t in range(4):
                    dve.wait_ge(xtr, t + 1)
                    for c in range(KC):
                        bank = 2 + 2 * (t % 2) + c // 4
                        last = v.tensor_scalar(m.hT[:, c, tile_cols(t)], psum[:, bank, 128 * (c % 4):128 * (c % 4) + 128],
                                               scale1[:, c, 0:1], shift1[:, c, 0:1], ALU.mult, ALU.add)
                    last.then_inc(hdone, 1)
                dve.wait_ge(xtr, NT)
                new = m.hT[:, :, SEQ:TOK].rearrange("p c (b s) -> p c b s", s=NS)
                for hf in range(2):
                    cs = slice(4 * hf, 4 * hf + 4)
                    for c in range(4 * hf, 4 * hf + 4):
                        src = psum[:, 2 + hf, 128 * (c % 4):128 * (c % 4) + 64].rearrange("p (b s) -> p b s", s=NS)
                        last = v.tensor_tensor(new[:, c], src, scale1[:, c, 1:9].unsqueeze(2).broadcast_to([128, NB, NS]), ALU.mult)
                last.then_inc(dv, 1)
                dve.wait_ge(dv, 4)
                for c in range(KC):
                    last = v.tensor_tensor(new[:, c], new[:, c], shift1[:, c, 1:9].unsqueeze(2).broadcast_to([128, NB, NS]), ALU.add)
                last.then_inc(hdone, 1)
                for j in range(4, 12):
                    add_bias(j)


def phase_gmlp(nc, m, ins, outs, st, psum):
    with ExitStack() as ctx:
        sb = lambda name, shape, dt=F32: ctx.enter_context(nc.sbuf_tensor(name, shape, dt))
        sem = ctx.enter_context(semaphores(nc))
        vn = sb("vn", [128, NT, D])
        lnw, lnb = sb("lnw", [128, D]), sb("lnb", [128, D])
        bsr = sb("bsr", [128, NG, 128])
        wst = sb("ws_prompt", [128, NG, 128])
        wsn = sb("ws_new", [64, NG, 64])
        wmT = sb("wmT_prompt", [128, NG, 128])
        wmTn = sb("wmT_new", [64, NG, 64])
        stats = sb("stats", [128, NT, 2, 6])
        mv = sb("meanvar", [128, NT, 2])
        rstd = sb("v_rstd", [128, NT])
        tmp = sb("sv_bias", [128, 2, TOK])
        wload, pload, cleared = sem("ws_loaded"), sem("lnp_loaded"), sem("ws_cleared")
        wtr, wmdone = sem("ws_tr"), sem("wmT_done")
        vmm, vev, umm, uev = sem("zv_mm"), sem("zv_ev"), sem("zu_mm"), sem("zu_ev")
        bst, mvd, rsd, vsc, vnd = sem("v_stats"), sem("mv_done"), sem("v_rstd_done"), sem("v_scaled"), sem("vn_done")
        smm, sbias, adone, vout = sem("sv_mm"), sem("sv_biased"), sem("a_done"), m.chunk_v_stored
        first = st.at["zv0"]
        with nc.Block() as block:
            @block.sync
            def _(sp):
                st.load(sp, first + 2, (vmm, 5))
                st.load(sp, first + 3, (vmm, 10))
                st.load(sp, first + 4, (umm, 4))
                st.load(sp, first + 5, (umm, 8))

            @block.gpsimd
            def _(pool):
                nc.gpsimd.memset(wsn[:, :, :], 0.0).then_inc(cleared, 1)
                nc.gpsimd.memset(mv[:, :, :], 1.0).then_inc(cleared, 1)
                pool.wait_ge(mvd, 1)
                nc.gpsimd.tensor_scalar(rstd[:, :], mv[:, :, 1], EPS, None, ALU.add).then_inc(rsd, 1)
                pool.wait_ge(rsd, 1)
                nc.gpsimd.tensor_tensor(rstd[:, :], rstd[:, :], m.half[:, 0:NT], ALU.pow).then_inc(rsd, 1)
                pool.wait_ge(pload, 48)
                for t in range(NT):
                    r = ROWS[t]
                    pool.wait_ge(vsc, 2 * t + 2)
                    nc.gpsimd.tensor_tensor(vn[0:r, t, :], vn[0:r, t, :], lnb[0:r, :], ALU.add).then_inc(vnd, 1)
                pool.wait_ge(vnd, NT)
                pool.dma_start(outs["chunk_v_sample"][0].rearrange("b s d -> (b s) d"), vn[0:64, 4, :]).then_inc(vout, 16)
                pool.wait_ge(vout, 16)

            @block.scalar
            def _(act):
                act.dma_start(wst[:, :, :], ins["w_s"][0].rearrange("g t s -> t g s")).then_inc(wload, 16)
                act.dma_start(lnw[:, :], ins["ln_v_w"][0].partition_broadcast(128)).then_inc(pload, 16)
                act.dma_start(lnb[:, :], ins["ln_v_b"][0].partition_broadcast(128)).then_inc(pload, 16)
                act.dma_start(bsr[:, :, :], ins["b_s"][0].partition_broadcast(128)).then_inc(pload, 16)
                act.wait_ge(cleared, 2)
                for b in range(NB):
                    act.dma_start(wsn[NS * b:NS * b + NS, :, NS * b:NS * b + NS],
                                  ins["w_s"][0, :, 0:NS, 0:NS].rearrange("g t s -> t g s")).then_inc(wload, 16)
                for j in range(2):
                    for t in range(NT):
                        act.wait_ge(vmm, NT * j + t + 1)
                        nc.scalar.activation(vn[0:ROWS[t], t, GW * j:GW * j + GW], psum[0:ROWS[t], (NT * j + t) % 2, :],
                                             ACT.Gelu).then_inc(vev, 1)
                for c in range(KC):
                    act.wait_ge(umm, c + 1)
                    for hf in range(2):
                        last = nc.scalar.activation(m.aT[:, c, HALF * hf:HALF * hf + HALF],
                                                    psum[:, 2 + 2 * (c % 2) + hf, 0:HALF], ACT.Gelu)
                    last.then_inc(uev, 1)

            @block.tensor
            def _(pe):
                pe.wait_ge(wload, 16 * (NB + 1))
                for g in range(NG):
                    nc.tensor.transpose(psum[:, 6, 128 * g:128 * g + 128], wst[:, g, :], m.ident[:, :])
                    last = nc.tensor.transpose(psum[0:64, 7, 64 * g:64 * g + 64], wsn[:, g, :], m.ident[0:64, 0:64])
                last.then_inc(wtr, 1)
                for j in range(2):
                    w = st.wait(pe, first + j)
                    for t in range(NT):
                        i = NT * j + t
                        if i >= 2:
                            pe.wait_ge(vev, i - 1)
                        for c in range(KC):
                            last = nc.tensor.matmul(psum[0:ROWS[t], i % 2, :], m.hT[:, c, tile_cols(t)], w[:, c, :],
                                                    start=c == 0, stop=c == KC - 1)
                        last.then_inc(vmm, 1)
                for c in range(KC):
                    if c % 4 == 0:
                        w = st.wait(pe, first + 2 + c // 4)
                    if c >= 2:
                        pe.wait_ge(uev, c - 1)
                    last = project(nc, psum, 2 + 2 * (c % 2), w, c % 4, m.hT)
                    last.then_inc(umm, 1)
                pe.wait_ge(wmdone, 2)
                pe.wait_ge(vnd, NT)
                pe.wait_ge(vev, 2 * NT)
                for c in range(KC):
                    if c >= 2:
                        pe.wait_ge(sbias, c - 1)
                    cs = slice(128 * c, 128 * c + 128)
                    for t in range(4):
                        nc.tensor.matmul(psum[:, c % 2, tile_cols(t)], vn[:, t, cs], wmT[:, c // 2, :], start=True, stop=True)
                    nc.tensor.matmul(psum[:, 6 + c % 2, 0:64], vn[0:64, 4, cs], wmTn[:, c // 2, :],
                                     start=True, stop=True).then_inc(smm, 1)

            @block.vector
            def _(dve):
                v = nc.vector
                dve.wait_ge(wtr, 1)
                v.tensor_tensor(wmT[:, :, :], psum[:, 6, :].rearrange("p (g t) -> p g t", g=NG),
                                m.cum[0][:, :].unsqueeze(1).broadcast_to([128, NG, 128]), ALU.mult).then_inc(wmdone, 1)
                v.tensor_tensor(wmTn[:, :, :], psum[0:64, 7, 0:256].rearrange("p (g t) -> p g t", g=NG),
                                m.cum[1][:, :].unsqueeze(1).broadcast_to([64, NG, 64]), ALU.mult).then_inc(wmdone, 1)
                dve.wait_ge(cleared, 2)
                for t in range(NT):
                    r = ROWS[t]
                    dve.wait_ge(vev, NT + t + 1)
                    for j in range(2):
                        last = v.bn_stats(stats[0:r, t, j, :], vn[0:r, t, GW * j:GW * j + GW])
                    last.then_inc(bst, 1)
                    dve.wait_ge(bst, t + 1)
                    last = v.bn_aggr(mv[0:r, t, :], stats[0:r, t, :, :])
                last.then_inc(mvd, 1)
                dve.wait_ge(mvd, 1)
                dve.wait_ge(rsd, 2)
                dve.wait_ge(pload, 48)
                for t in range(NT):
                    r = ROWS[t]
                    v.tensor_scalar(vn[0:r, t, :], vn[0:r, t, :], mv[0:r, t, 0:1], rstd[0:r, t:t + 1],
                                    ALU.subtract, ALU.mult).then_inc(vsc, 1)
                    dve.wait_ge(vsc, 2 * t + 1)
                    v.tensor_tensor(vn[0:r, t, :], vn[0:r, t, :], lnw[0:r, :], ALU.mult).then_inc(vsc, 1)
                for c in range(KC):
                    g, k = c // 2, c % 2
                    dve.wait_ge(smm, c + 1)
                    if c >= 2:
                        dve.wait_ge(adone, c - 1)
                    v.tensor_tensor(tmp[:, k, 0:SEQ].rearrange("p (t s) -> p t s", s=128),
                                    psum[:, k, :].rearrange("p (t s) -> p t s", s=128),
                                    bsr[:, g, :].unsqueeze(1).broadcast_to([128, 4, 128]), ALU.add)
                    v.tensor_tensor(tmp[:, k, SEQ:TOK].rearrange("p (b s) -> p b s", s=NS),
                                    psum[:, 6 + k, 0:64].rearrange("p (b s) -> p b s", s=NS),
                                    bsr[:, g, 0:NS].unsqueeze(1).broadcast_to([128, NB, NS]), ALU.add).then_inc(sbias, 1)
                    dve.wait_ge(sbias, c + 1)
                    dve.wait_ge(uev, c + 1)
                    v.tensor_tensor(m.aT[:, c, :], m.aT[:, c, :], tmp[:, k, :], ALU.mult).then_inc(adone, 1)


def project(nc, psum, bank, w, q, x):
    for hf in range(2):
        for c in range(KC):
            last = nc.tensor.matmul(psum[:, bank + hf, 0:HALF], w[:, c, 128 * q:128 * q + 128],
                                    x[:, c, HALF * hf:HALF * hf + HALF], start=c == 0, stop=c == KC - 1)
    return last


def phase_qkv(nc, m, ins, outs, st, psum):
    with ExitStack() as ctx:
        sb = lambda name, shape, dt=F32: ctx.enter_context(nc.sbuf_tensor(name, shape, dt))
        sem = ctx.enter_context(semaphores(nc))
        zst = sb("z_staged", [128, 2, PST + NB * SST])
        y = sb("conv_y", [128, 2, TOK])
        sc = sb("state_rows", [NB * HIST, NCH * 128])
        scT = sb("state_T", [128, NCH, NB * HIST])
        cst = sb("conv_last", [128, NCH, HIST * (NB + 1)])
        cout = sb("conv_out", [HIST * (NB + 1), NCH * 128])
        sqb = sb("qk_sq", [128, 512])
        sqn = sb("qk_sq_new", [64, 128])
        baT = sb("baT", [16, TOK])
        scl, sctr, scd = sem("state_loaded"), sem("state_tr"), sem("stateT_done")
        zmm, zev, hist, taken = sem("z_mm"), sem("z_ev"), sem("hist_staged"), sem("last_taken")
        cstep, conv, silu = sem("conv_step"), sem("conv_done"), sem("silu_done")
        qtr, qsq, qred = sem("qk_tr"), sem("qk_squared"), sem("qk_reduced")
        batr, bad, zzd = sem("ba_tr"), sem("ba_done"), sem("zz_done")
        otr, oev, ost, ssinit = sem("last_tr"), sem("last_ev"), m.conv_stored, sem("ss_init")
        first = st.at["qkv0"]
        BA = NCH
        stage = lambda c: zst[:, c % 2, :]
        newz = lambda c: zst[:, c % 2, PST:].rearrange("p (b s) -> p b s", s=SST)
        newy = lambda c: y[:, c % 2, SEQ:].rearrange("p (b s) -> p b s", s=NS)
        with nc.Block() as block:
            @block.sync
            def _(sp):
                for i in range(6):
                    st.load(sp, first + 2 + i, (zmm, 4 * i + 4))
                st.load(sp, first + 8, (zmm, BA + 1))
                st.load(sp, first + 9, (zmm, BA + 5))
                st.load(sp, first + 10, (zmm, BA + 9))
                sp.wait_ge(oev, 6)
                sp.dma_start(outs["conv_prompt"][0, 0], cout[0:HIST, :]).then_inc(ost, 16)
                sp.dma_start(outs["conv_sample"][0].rearrange("b j c -> (b j) c"), cout[HIST:, :]).then_inc(ost, 16)
                sp.wait_ge(ost, 32)

            @block.gpsimd
            def _(pool):
                nc.gpsimd.memset(m.ss[:, :, :], 1.0).then_inc(ssinit, 1)
                nc.gpsimd.memset(m.ba[:, :, :], 0.0).then_inc(ssinit, 1)
                for c in range(2):
                    nc.gpsimd.memset(zst[:, c, 0:HIST], 0.0)
                pool.wait_ge(scd, 1)
                for c in range(NCH):
                    if c >= 2:
                        pool.wait_ge(conv, c - 1)
                    nc.gpsimd.tensor_copy(newz(c)[:, :, 0:HIST], scT[:, c, :].rearrange("p (b j) -> p b j", j=HIST)).then_inc(hist, 1)
                    pool.wait_ge(zev, c + 1)
                    nc.gpsimd.tensor_copy(cst[:, c, 0:HIST], zst[:, c % 2, SEQ:SEQ + HIST])
                    nc.gpsimd.tensor_copy(cst[:, c, HIST:].rearrange("p (b j) -> p b j", j=HIST),
                                          newz(c)[:, :, NS:NS + HIST]).then_inc(taken, 1)
                for c in range(H):
                    pool.wait_ge(zev, BA + 2 + c)
                    nc.gpsimd.tensor_scalar(m.zzT[:, c, :], m.zzT[:, c, :], m.convT[:, 96:97], None, ALU.mult).then_inc(zzd, 1)

            @block.scalar
            def _(act):
                act.dma_start(sc[:, :], ins["state_conv"][0].rearrange("b j c -> (b j) c")).then_inc(scl, 16)

                def evacuate(c):
                    act.wait_ge(zmm, c + 1)
                    if c >= 2:
                        act.wait_ge(conv, c - 1)
                        act.wait_ge(taken, c - 1)
                    b = 2 * (c % 2)
                    nc.scalar.copy(stage(c)[:, HIST:HIST + HALF], psum[:, b, 0:HALF])
                    nc.scalar.copy(stage(c)[:, HIST + HALF:PST], psum[:, b + 1, 0:SEQ - HALF])
                    nc.scalar.copy(newz(c)[:, :, HIST:], psum[:, b + 1, SEQ - HALF:HALF].rearrange("p (b s) -> p b s", s=NS)).then_inc(zev, 1)

                def apply_silu(c):
                    act.wait_ge(conv, c + 1)
                    nc.scalar.activation(m.qkvT[:, c, :], y[:, c % 2, :], ACT.Silu).then_inc(silu, 1)

                def square(c):
                    act.wait_ge(qtr, c + 1)
                    if c:
                        act.wait_ge(qred, c)
                    nc.scalar.activation(sqb[:, :], psum[:, 4, :], ACT.Square)
                    nc.scalar.activation(sqn[:, :], psum[0:64, 5, 0:128], ACT.Square).then_inc(qsq, 1)

                for c in range(NCH):
                    evacuate(c)
                    if c >= 1:
                        apply_silu(c - 1)
                    if 2 <= c < 18:
                        square(c - 2)
                apply_silu(NCH - 1)
                act.wait_ge(zmm, BA + 1)
                for hf in range(2):
                    last = nc.scalar.copy(baT[:, HALF * hf:HALF * hf + HALF], psum[0:16, hf, 0:HALF])
                last.then_inc(zev, 1)
                for c in range(H):
                    n = BA + 1 + c
                    act.wait_ge(zmm, n + 1)
                    for hf in range(2):
                        last = nc.scalar.activation(m.zzT[:, c, HALF * hf:HALF * hf + HALF], psum[:, 2 * (n % 2) + hf, 0:HALF], ACT.Silu)
                    last.then_inc(zev, 1)

            @block.tensor
            def _(pe):
                pe.wait_ge(scl, 16)
                for c in range(NCH):
                    last = nc.tensor.transpose(psum[:, 6 + c // 12, 24 * (c % 12):24 * (c % 12) + 24],
                                               sc[:, 128 * c:128 * c + 128], m.ident[0:24, 0:24])
                last.then_inc(sctr, 1)
                for c in range(NCH):
                    if c % 4 == 0:
                        w = st.wait(pe, first + c // 4)
                    if c >= 2:
                        pe.wait_ge(zev, c - 1)
                    project(nc, psum, 2 * (c % 2), w, c % 4, m.hT).then_inc(zmm, 1)
                    if 2 <= c < 18:
                        pe.wait_ge(silu, c - 1)
                        if c >= 3:
                            pe.wait_ge(qsq, c - 2)
                        for t in range(NT):
                            last = nc.tensor.transpose(psum[0:ROWS[t], 4 + t // 4, 128 * (t % 4):128 * (t % 4) + 128],
                                                       m.qkvT[:, c - 2, tile_cols(t)], m.ident[:, :])
                        last.then_inc(qtr, 1)
                w = st.wait(pe, first + 6)
                pe.wait_ge(zev, BA - 1)
                for hf in range(2):
                    for c in range(KC):
                        last = nc.tensor.matmul(psum[0:16, hf, 0:HALF], w[:, c, 0:16], m.hT[:, c, HALF * hf:HALF * hf + HALF],
                                                start=c == 0, stop=c == KC - 1)
                last.then_inc(zmm, 1)
                for c in range(H):
                    n = BA + 1 + c
                    if c % 4 == 0:
                        w = st.wait(pe, first + 7 + c // 4)
                    pe.wait_ge(zev, n - 1)
                    project(nc, psum, 2 * (n % 2), w, c % 4, m.hT).then_inc(zmm, 1)
                pe.wait_ge(qsq, 16)
                for t in range(NT):
                    last = nc.tensor.transpose(psum[0:ROWS[t], 4, 16 * t:16 * t + 16], baT[:, tile_cols(t)], m.ident[0:16, 0:16])
                last.then_inc(batr, 1)
                pe.wait_ge(taken, NCH)
                pe.wait_ge(scd, 1)
                for r in range(6):
                    if r >= 2:
                        pe.wait_ge(oev, r - 1)
                    for q in range(4):
                        last = nc.tensor.transpose(psum[0:27, 6 + r % 2, 128 * q:128 * q + 128], cst[:, 4 * r + q, :], m.ident[:, :])
                    last.then_inc(otr, 1)

            @block.vector
            def _(dve):
                v = nc.vector
                dve.wait_ge(sctr, 1)
                v.tensor_copy(scT[:, 0:12, :].rearrange("p c r -> p (c r)"), psum[:, 6, 0:288])
                v.tensor_copy(scT[:, 12:24, :].rearrange("p c r -> p (c r)"), psum[:, 7, 0:288]).then_inc(scd, 1)
                dve.wait_ge(ssinit, 2)

                def reduce(c):
                    dve.wait_ge(qsq, c + 1)
                    v.tensor_reduce(m.ss[:, 0:4, c], sqb[:, :].rearrange("p (t f) -> p t f", t=4), AX.X, ALU.add)
                    v.tensor_reduce(m.ss[0:64, 4, c:c + 1], sqn[:, :], AX.X, ALU.add).then_inc(qred, 1)

                for c in range(NCH):
                    dve.wait_ge(zev, c + 1)
                    dve.wait_ge(hist, c + 1)
                    if c >= 2:
                        dve.wait_ge(silu, c - 1)
                    for j in range(HIST + 1):
                        w = m.convT[:, NCH * j + c:NCH * j + c + 1]
                        pz, nz = stage(c)[:, j:j + SEQ], newz(c)[:, :, j:j + NS]
                        py, ny = y[:, c % 2, 0:SEQ], newy(c)
                        if j == 0:
                            v.tensor_scalar(py, pz, w, None, ALU.mult)
                            v.tensor_scalar(ny, nz, w, None, ALU.mult).then_inc(cstep, 1)
                        else:
                            dve.wait_ge(cstep, 3 * c + j)
                            v.scalar_tensor_tensor(py, pz, w, py, ALU.mult, ALU.add)
                            v.scalar_tensor_tensor(ny, nz, w, ny, ALU.mult, ALU.add).then_inc(cstep if j < HIST else conv, 1)
                    if 3 <= c < 19:
                        reduce(c - 3)
                dve.wait_ge(batr, 1)
                v.tensor_copy(m.ba[:, 0:4, :].rearrange("p t r -> p (t r)"), psum[:, 4, 0:64])
                v.tensor_copy(m.ba[0:64, 4, :], psum[0:64, 4, 64:80]).then_inc(bad, 1)
                for r in range(6):
                    dve.wait_ge(otr, r + 1)
                    v.tensor_copy(cout[:, 512 * r:512 * r + 512], psum[0:27, 6 + r % 2, :]).then_inc(oev, 1)


def phase_delta(nc, m, ins, outs, psum):
    with ExitStack() as ctx:
        sb = lambda name, shape, dt=F32: ctx.enter_context(nc.sbuf_tensor(name, shape, dt))
        sem = ctx.enter_context(semaphores(nc))
        two = lambda name: [sem(f"{name}_{g}") for g in range(2)]
        small = lambda name: sb(name, [128, NT, H])
        beta, g_, gc, gt, egc, kdec, egl = (small(n) for n in ("beta", "g", "gc", "gt", "egc", "kdec", "egl"))
        vbs, nbk, nbe, cq, cq2 = (small(n) for n in ("vbs", "nbk", "nbe", "cq", "cq2"))
        xa, ax = small("xa"), small("ax")
        rr = sb("rr", [128, NT, 16])
        dtb, alog = sb("dtb", [128, H]), sb("alog", [128, H])
        egn = sb("egl_new", [128, H, NB])
        ms, fo = sb("ms", [128, 2, 4]), sb("fo", [128, 2, 4])
        S = sb("S", [128, H, 128])
        S0 = sb("S0", [128, 2, NB, 128])
        mat = lambda name: sb(name, [128, 2, 4, 128])
        Dd, Dm, nL, W, at, atT, vb, kd, on = (mat(n) for n in ("decay", "decay_low", "negL", "W", "attn", "attnT", "vb", "kd", "o_norm"))
        TU = sb("TU", [128, 2, 2, 4, 128])
        ploaded, prep, pprep, init = sem("dp_loaded"), sem("prep"), sem("prep_pool"), sem("d_init")
        aprep, gmm, nprep = sem("prep_act"), sem("g_mm"), sem("prep_done")
        (grow, ktr, vtr, gram, attn, attr, u1tr, wmm, ymm, ttr, ks, qs, vp, av, ds, otr) = (
            two(n) for n in ("grow", "ktr", "vtr", "gram", "attn_mm", "attn_tr", "u1_tr", "w_mm", "y_mm", "t_tr", "ks", "qs", "vp", "av", "ds", "o_tr"))
        (ed, nl, tcopy, t1, atd, uup, rd, od, sd, v2, zd) = (
            two(n) for n in ("e", "negL_done", "t_ident", "t1", "attn_done", "u_upd", "r_done", "o_done", "s_done", "var", "zz_mult"))
        (dd, kdd, vbd, attd, u1, wcp, tcp, o1, vnd, sqd, ond, kqc) = (
            two(n) for n in ("d_exp", "kd_done", "vb_done", "attnT_done", "u1_done", "w_copy", "t_copy", "o1", "vn_done", "o_sq", "on_done", "kq_copy"))
        dm, fod, kqt = two("dm"), two("fo_done"), two("kq_tr")
        fstep = sem("fo_step")
        egnd, s0use, vxd, smul, sadd, dsn = sem("egn_done"), sem("s0_used"), sem("vx_done"), sem("s0_scaled"), sem("s0_added"), sem("ds_new")
        s0ld, s0st, sst = [sem(f"s0_loaded{i}") for i in range(2)], [m.delta0_stored, m.delta1_stored], m.delta_p_stored
        T = lambda g: TU[:, g, 0]
        U = lambda g: TU[:, g, 1]
        bank = lambda g, k: psum[:, 4 * g + k, :].rearrange("p (h c) -> p h c", h=4)
        A, B, C, X = 0, 1, 2, 3
        LV = [6] * 4 + [2]
        base = [6 * t for t in range(NT)]
        tbase = [5 * t for t in range(NT)]
        G2 = range(2)
        qT = lambda t, hh: m.qkvT[:, hh, tile_cols(t)]
        kT = lambda t, hh: m.qkvT[:, H + hh, tile_cols(t)]
        vT = lambda t, hh: m.qkvT[:, 2 * H + hh, tile_cols(t)]
        col = lambda x, t, hh, r: x[0:r, t, hh:hh + 1]

        def mask(l, r):
            return m.level[0:r, l, 0:r].bitcast(U16).unsqueeze(1).broadcast_to([r, 4, r])

        with nc.Block() as block:
            @block.sync
            def _(sp):
                sp.dma_start(dtb[:, :], ins["dt_bias"][0].partition_broadcast(128)).then_inc(ploaded, 16)
                sp.dma_start(alog[:, :], ins["a_log"][0].partition_broadcast(128)).then_inc(ploaded, 16)
                for n in range(8):
                    if n >= 2:
                        sp.wait_ge(s0use, n - 1)
                    sp.dma_start(S0[:, n % 2], ins["state_delta"][0, :, n].rearrange("b k v -> k b v")).then_inc(s0ld[n % 2], 16)
                for g in G2:
                    sp.wait_ge(sd[g], 4)
                    sp.dma_start(outs["delta_prompt"][0, 0, 4 * g:4 * g + 4].rearrange("h k v -> k h v"), S[:, 4 * g:4 * g + 4]).then_inc(sst, 16)
                for i in range(8):
                    sp.wait_ge(s0use, min(7 + i, 8))
                    if i >= 2:
                        sp.wait_ge(sadd, i - 1)
                        hh = 4 * (i % 2) + (i - 2) // 2
                        sp.dma_start(outs["delta_sample"][0, :, hh].rearrange("b k v -> k b v"), S0[:, i % 2]).then_inc(s0st[i % 2], 16)
                        sp.wait_ge(s0st[i % 2], 16 * (i // 2))
                    hh = 4 * (i % 2) + i // 2
                    sp.dma_start(S0[:, i % 2], ins["state_delta"][0, :, hh].rearrange("b k v -> k b v")).then_inc(s0ld[i % 2], 16)
                for i in (8, 9):
                    sp.wait_ge(sadd, i - 1)
                    hh = 4 * (i % 2) + (i - 2) // 2
                    sp.dma_start(outs["delta_sample"][0, :, hh].rearrange("b k v -> k b v"), S0[:, i % 2]).then_inc(s0st[i % 2], 16)
                sp.wait_ge(s0st[0], 64)
                sp.wait_ge(s0st[1], 64)
                sp.wait_ge(sst, 32)

            @block.gpsimd
            def _(pool):
                p = nc.gpsimd
                for x in (gc, gt):
                    p.memset(x[:, :, :], 0.0).then_inc(init, 1)
                p.memset(S[:, :, :], 0.0).then_inc(init, 1)
                n = [0]

                def step(i):
                    n[0] += 1
                    i.then_inc(pprep, 1)
                    pool.wait_ge(pprep, n[0])
                step(p.tensor_scalar(rr[:, :, :], m.ss[:, :, :], EPS, None, ALU.add))
                step(p.tensor_tensor(rr[:, :, :].rearrange("p t r -> p (t r)"), rr[:, :, :].rearrange("p t r -> p (t r)"), m.half[:, :], ALU.pow))
                rq, rk = rr[:, :, 0:H], rr[:, :, H:2 * H]
                step(p.tensor_scalar(cq[:, :, :], rq, 128 ** -0.5, None, ALU.mult))
                step(p.tensor_tensor(cq2[:, :, :], cq[:, :, :], cq[:, :, :], ALU.mult))
                step(p.tensor_scalar(cq2[:, :, :], cq2[:, :, :], 1.0 / 128, None, ALU.mult))
                pool.wait_ge(aprep, 1)
                step(p.tensor_tensor(vbs[:, :, :], beta[:, :, :], rk, ALU.mult))
                step(p.tensor_tensor(nbk[:, :, :], vbs[:, :, :], rk, ALU.mult))
                step(p.tensor_scalar(nbk[:, :, :], nbk[:, :, :], -1.0, None, ALU.mult))
                pool.wait_ge(aprep, 7)
                p.tensor_tensor(nbe[:, :, :], nbk[:, :, :], egc[:, :, :], ALU.mult).then_inc(nprep, 1)
                k = 0
                for t in range(NT):
                    r = ROWS[t]
                    low = m.low[t // 4][:, :].unsqueeze(1).broadcast_to([r, 4, r])
                    for g in G2:
                        pool.wait_ge(dd[g], t + 1)
                        if t:
                            pool.wait_ge(atd[g], t)
                        p.tensor_tensor(Dm[0:r, g, :, 0:r], Dd[0:r, g, :, 0:r], low, ALU.mult).then_inc(dm[g], 1)
                    if t == 4:
                        for i in range(8):
                            g, h = i % 2, i // 2
                            pool.wait_ge(vnd[g], NT)
                            if i >= 2:
                                pool.wait_ge(dsn, i - 1)
                            p.tensor_tensor(TU[0:64, g].rearrange("p a b c -> p (a b) c"), Dd[0:64, g, h, :].unsqueeze(1).broadcast_to([64, NB, 128]),
                                            m.blk[1][:, 0:64:NS].unsqueeze(2).broadcast_to([64, NB, 128]), ALU.mult).then_inc(vxd, 1)
                            pool.wait_ge(s0ld[i % 2], 16 * (4 + i // 2 + 1))
                            pool.wait_ge(egnd, 2)
                            hh = 4 * g + h
                            p.tensor_tensor(S0[:, i % 2], S0[:, i % 2], egn[:, hh, :].unsqueeze(2).broadcast_to([128, NB, 128]),
                                            ALU.mult).then_inc(smul, 1)
                    for g in G2:
                        pool.wait_ge(v2[g], t + 1)
                        f = fo[0:r, g, :]
                        p.tensor_scalar(f, ms[0:r, g, :], EPS, None, ALU.add).then_inc(fstep, 1)
                        pool.wait_ge(fstep, k + 1)
                        p.tensor_tensor(f, f, m.half[0:r, 0:4], ALU.pow).then_inc(fstep, 1)
                        pool.wait_ge(fstep, k + 2)
                        p.tensor_tensor(f, f, cq[0:r, t, 4 * g:4 * g + 4], ALU.mult).then_inc(fod[g], 1)
                        k += 2

            @block.scalar
            def _(act):
                a = nc.scalar
                a.activation(beta[:, :, :], m.ba[:, :, 0:H], ACT.Sigmoid).then_inc(aprep, 1)
                act.wait_ge(prep, 1)
                a.activation(ax[:, :, :], xa[:, :, :], ACT.Abs).then_inc(aprep, 1)
                act.wait_ge(aprep, 2)
                a.activation(ax[:, :, :], ax[:, :, :], ACT.Exp, scale=-1.0).then_inc(aprep, 1)
                act.wait_ge(aprep, 3)
                a.activation(ax[:, :, :], ax[:, :, :], ACT.Ln, bias=1.0).then_inc(aprep, 1)
                act.wait_ge(ploaded, 32)
                a.activation(alog[:, :], alog[:, :], ACT.Exp).then_inc(aprep, 1)
                act.wait_ge(prep, 5)
                a.activation(kdec[:, :, :], kdec[:, :, :], ACT.Exp).then_inc(aprep, 1)
                a.activation(egc[:, :, :], gc[:, :, :], ACT.Exp).then_inc(aprep, 1)
                a.activation(egl[:, :, :], gt[:, :, :], ACT.Exp).then_inc(aprep, 1)
                act.wait_ge(nprep, 1)
                act.wait_ge(aprep, 8)
                act.wait_ge(pprep, 8)
                for t in range(NT):
                    r = ROWS[t]
                    for g in G2:
                        act.wait_ge(ed[g], t + 1)
                        a.activation(Dd[0:r, g, :, 0:r], Dd[0:r, g, :, 0:r], ACT.Exp, scale=-1.0).then_inc(dd[g], 1)
                        if t == 4:
                            a.activation(egn[:, 4 * g:4 * g + 4, :], bank(g, A)[:, :, NS - 1:64:NS], ACT.Exp).then_inc(egnd, 1)
                    for g in G2:
                        act.wait_ge(ktr[g], t + 1)
                        for h in range(4):
                            last = a.activation(kd[0:r, g, h, :], bank(g, B)[0:r, h, :], ACT.Copy, scale=col(kdec, t, 4 * g + h, r))
                        last.then_inc(kdd[g], 1)
                        act.wait_ge(vtr[g], t + 1)
                        if t:
                            act.wait_ge(rd[g], t)
                        for h in range(4):
                            last = a.activation(vb[0:r, g, h, :], bank(g, C)[0:r, h, :], ACT.Copy, scale=col(vbs, t, 4 * g + h, r))
                        last.then_inc(vbd[g], 1)
                    for g in G2:
                        act.wait_ge(attr[g], t + 1)
                        a.copy(atT[0:r, g, :, 0:r], bank(g, B)[0:r, :, 0:r]).then_inc(attd[g], 1)
                    for g in G2:
                        act.wait_ge(u1tr[g], t + 1)
                        a.copy(U(g)[0:r, :, 0:r], bank(g, C)[0:r, :, 0:r]).then_inc(u1[g], 1)
                    for l in range(1, LV[t] + 1):
                        for g in G2:
                            act.wait_ge(wmm[g], base[t] + l)
                            a.copy(W[0:r, g, :, 0:r], bank(g, X)[0:r, :, 0:r]).then_inc(wcp[g], 1)
                        if l < LV[t]:
                            for g in G2:
                                act.wait_ge(ttr[g], tbase[t] + l)
                                a.copy(T(g)[0:r, :, 0:r], bank(g, B)[0:r, :, 0:r]).then_inc(tcp[g], 1)
                    if t == 4:
                        for g in G2:
                            act.wait_ge(ks[g], NT)
                            act.wait_ge(attr[g], NT)
                            for half in range(2):
                                last = a.copy(at[:, g].rearrange("p h (a x) -> p h a x", a=2)[:, :, half].rearrange("p h (b s) -> p h b s", s=NS),
                                              psum[:, 4 * g + C, :].rearrange("p (h b a s) -> p h b a s", h=4, b=NB, a=2)[:, :, :, half])
                            last.then_inc(kqc[g], 1)
                    for g in G2:
                        act.wait_ge(qs[g], t + 1)
                        if t:
                            act.wait_ge(otr[g], t)
                        for h in range(4):
                            last = a.activation(on[0:r, g, h, :], bank(g, X)[0:r, h, :], ACT.Copy, scale=col(egc, t, 4 * g + h, r))
                        last.then_inc(o1[g], 1)
                    for g in G2:
                        act.wait_ge(vp[g], t + 1)
                        act.wait_ge(dm[g], t + 1)
                        a.copy(Dd[0:r, g, :, :], bank(g, A)[0:r, :, :]).then_inc(vnd[g], 1)
                    for g in G2:
                        act.wait_ge(od[g], t + 1)
                        a.activation(at[0:r, g], on[0:r, g], ACT.Square).then_inc(sqd[g], 1)
                    for g in G2:
                        act.wait_ge(fod[g], t + 1)
                        act.wait_ge(sqd[g], t + 1)
                        for h in range(4):
                            last = a.activation(on[0:r, g, h, :], on[0:r, g, h, :], ACT.Copy, scale=fo[0:r, g, h:h + 1])
                        last.then_inc(ond[g], 1)

            @block.tensor
            def _(pe):
                te = nc.tensor
                pe.wait_ge(prep, 3)
                pe.wait_ge(init, 3)
                for k, x in ((0, m.cum), (1, m.blk)):
                    te.matmul(psum[:, k, 0:32], x[0][:, :], g_[:, 0:4, :].rearrange("p t h -> p (t h)"), start=True, stop=True)
                    last = te.matmul(psum[0:64, k, 32:40], x[1][:, :], g_[0:64, 4, :], start=True, stop=True)
                last.then_inc(gmm, 1)
                pe.wait_ge(prep, 5)

                def out_transposes(t):
                    r = ROWS[t]
                    for g in G2:
                        pe.wait_ge(ond[g], t + 1)
                        for h in range(4):
                            last = te.transpose(bank(g, X)[:, h, 0:r], on[0:r, g, h, :], m.ident[0:r, 0:r])
                        last.then_inc(otr[g], 1)

                for t in range(NT):
                    r = ROWS[t]
                    cum = m.cum[t // 4]
                    for g in G2:
                        if t:
                            pe.wait_ge(vnd[g], t)
                        for h in range(4):
                            hh = 4 * g + h
                            last = te.matmul(bank(g, A)[:, h, 0:r], g_[0:r, t, hh:hh + 1].to_broadcast([r, 128]), cum[:, :], start=True, stop=True)
                        last.then_inc(grow[g], 1)
                    for g in G2:
                        if t:
                            pe.wait_ge(od[g], t)
                        for h in range(4):
                            last = te.transpose(bank(g, B)[0:r, h, :], kT(t, 4 * g + h), m.ident[:, :])
                        last.then_inc(ktr[g], 1)
                        if t:
                            pe.wait_ge(sd[g], t)
                        for h in range(4):
                            last = te.transpose(bank(g, C)[0:r, h, :], vT(t, 4 * g + h), m.ident[:, :])
                        last.then_inc(vtr[g], 1)
                    if t:
                        out_transposes(t - 1)
                    for g in G2:
                        if t:
                            pe.wait_ge(zd[g], t)
                        for h in range(4):
                            last = te.matmul(bank(g, X)[0:r, h, 0:r], kT(t, 4 * g + h), kT(t, 4 * g + h), start=True, stop=True)
                        last.then_inc(gram[g], 1)
                        pe.wait_ge(ed[g], t + 1)
                        if t == 4:
                            pe.wait_ge(egnd, g + 1)
                        for h in range(4):
                            last = te.matmul(bank(g, A)[0:r, h, 0:r], qT(t, 4 * g + h), kT(t, 4 * g + h), start=True, stop=True)
                        last.then_inc(attn[g], 1)
                    for g in G2:
                        pe.wait_ge(atd[g], t + 1)
                        pe.wait_ge(kdd[g], t + 1)
                        for h in range(4):
                            last = te.transpose(bank(g, B)[0:r, h, 0:r], at[0:r, g, h, 0:r], m.ident[0:r, 0:r])
                        last.then_inc(attr[g], 1)
                    for g in G2:
                        pe.wait_ge(t1[g], t + 1)
                        pe.wait_ge(vbd[g], t + 1)
                        for h in range(4):
                            last = te.transpose(bank(g, C)[0:r, h, 0:r], T(g)[0:r, h, 0:r], m.ident[0:r, 0:r])
                        last.then_inc(u1tr[g], 1)
                    for l in range(1, LV[t] + 1):
                        for g in G2:
                            if l == 1:
                                pe.wait_ge(u1[g], t + 1)
                            else:
                                pe.wait_ge(uup[g], base[t] + l - 1)
                            for h in range(4):
                                last = te.matmul(bank(g, X)[0:r, h, 0:r], nL[0:r, g, h, 0:r], U(g)[0:r, h, 0:r], start=True, stop=True)
                            last.then_inc(wmm[g], 1)
                        for g in G2:
                            pe.wait_ge(wcp[g], base[t] + l)
                            if l > 1:
                                pe.wait_ge(tcp[g], tbase[t] + l - 1)
                            for h in range(4):
                                last = te.matmul(bank(g, A)[0:r, h, 0:r], T(g)[0:r, h, 0:r], W[0:r, g, h, 0:r], start=True, stop=True)
                            last.then_inc(ymm[g], 1)
                        if l < LV[t]:
                            for g in G2:
                                pe.wait_ge(uup[g], base[t] + l)
                                pe.wait_ge(attd[g], t + 1)
                                for h in range(4):
                                    last = te.transpose(bank(g, B)[0:r, h, 0:r], U(g)[0:r, h, 0:r], m.ident[0:r, 0:r])
                                last.then_inc(ttr[g], 1)
                    if t < 4:
                        for g in G2:
                            if t:
                                pe.wait_ge(sd[g], t)
                            for h in range(4):
                                last = te.matmul(bank(g, C)[:, h, :], kT(t, 4 * g + h), S[:, 4 * g + h, :], start=True, stop=True)
                            last.then_inc(ks[g], 1)
                            for h in range(4):
                                last = te.matmul(bank(g, X)[:, h, :], qT(t, 4 * g + h), S[:, 4 * g + h, :], start=True, stop=True)
                            last.then_inc(qs[g], 1)
                    else:
                        for g in G2:
                            for h in range(4):
                                hh = 4 * g + h
                                pe.wait_ge(s0ld[hh % 2], 16 * (hh // 2 + 1))
                                for b in range(NB):
                                    last = te.matmul(psum[:, 4 * g + C, 128 * h + 16 * b:128 * h + 16 * b + 16], S0[:, hh % 2, b, :],
                                                     m.qkvT[:, hh:hh + H + 1:H, SEQ + NS * b:SEQ + NS * b + NS], start=True, stop=True)
                                last.then_inc(s0use, 1)
                            te.transpose(bank(g, B)[0:64, 0, 0:64], m.ident[0:64, 0:64], m.ident[0:64, 0:64]).then_inc(ks[g], 1)
                        for g in G2:
                            pe.wait_ge(kqc[g], 1)
                            for h in range(4):
                                te.transpose(bank(g, X)[0:64, h, :], at[:, g, h, 0:64], m.ident[:, :])
                                last = te.transpose(bank(g, B)[0:64, h, :], at[:, g, h, 64:128], m.ident[:, :])
                            last.then_inc(qs[g], 1)
                    for g in G2:
                        pe.wait_ge(rd[g], t + 1)
                        pe.wait_ge(uup[g], base[t] + LV[t])
                        for h in range(4):
                            last = te.matmul(bank(g, A)[0:r, h, :], U(g)[0:r, h, 0:r], W[0:r, g, h, :], start=True, stop=True)
                        last.then_inc(vp[g], 1)
                    for g in G2:
                        pe.wait_ge(vnd[g], t + 1)
                        for h in range(4):
                            last = te.matmul(bank(g, B)[0:r, h, :], atT[0:r, g, h, 0:r], Dd[0:r, g, h, :], start=True, stop=True)
                        last.then_inc(av[g], 1)
                        if t < 4:
                            for h in range(4):
                                last = te.matmul(bank(g, C)[:, h, :], kd[:, g, h, :], Dd[:, g, h, :], start=True, stop=True)
                            last.then_inc(ds[g], 1)
                for i in range(8):
                    g, h = i % 2, i // 2
                    pe.wait_ge(vxd, i + 1)
                    pe.wait_ge(o1[g], NT)
                    if i >= 2:
                        pe.wait_ge(sadd, i - 1)
                    for hf in range(2):
                        last = te.matmul(psum[:, 4 * g + C + hf, :], kd[0:64, g, h, :], TU[0:64, g, hf].rearrange("p a b -> p (a b)"), start=True, stop=True)
                    last.then_inc(dsn, 1)
                pe.wait_ge(sadd, 8)
                out_transposes(4)

            @block.vector
            def _(dve):
                v = nc.vector
                dve.wait_ge(ploaded, 32)
                bc = lambda x: x[:, :].unsqueeze(1).broadcast_to([128, NT, H])
                v.tensor_tensor(xa[:, :, :], m.ba[:, :, H:2 * H], bc(dtb), ALU.add).then_inc(prep, 1)
                dve.wait_ge(prep, 1)
                dve.wait_ge(aprep, 5)
                v.scalar_tensor_tensor(xa[:, :, :], xa[:, :, :], 0.0, ax[:, :, :], ALU.max, ALU.add).then_inc(prep, 1)
                dve.wait_ge(prep, 2)
                v.scalar_tensor_tensor(g_[:, :, :], xa[:, :, :], -1.0, bc(alog), ALU.mult, ALU.mult).then_inc(prep, 1)
                dve.wait_ge(gmm, 1)
                dve.wait_ge(init, 3)
                for k, x in ((0, gc), (1, gt)):
                    v.tensor_copy(x[:, 0:4, :].rearrange("p t h -> p (t h)"), psum[:, k, 0:32])
                    last = v.tensor_copy(x[0:64, 4, :], psum[0:64, k, 32:40])
                last.then_inc(prep, 1)
                dve.wait_ge(prep, 4)
                v.tensor_tensor(kdec[:, :, :], gt[:, :, :], gc[:, :, :], ALU.subtract).then_inc(prep, 1)
                dve.wait_ge(nprep, 1)
                dve.wait_ge(aprep, 8)
                dve.wait_ge(pprep, 8)

                def gate(t):
                    r = ROWS[t]
                    for g in G2:
                        dve.wait_ge(otr[g], t + 1)
                        z = m.zzT[:, 4 * g:4 * g + 4, tile_cols(t)]
                        v.tensor_tensor(z, z, bank(g, X)[:, :, 0:r], ALU.mult).then_inc(zd[g], 1)

                for t in range(NT):
                    r = ROWS[t]
                    for g in G2:
                        dve.wait_ge(grow[g], t + 1)
                        if t:
                            dve.wait_ge(ds[g], t)
                        for h in range(4):
                            last = v.tensor_scalar(Dd[0:r, g, h, 0:r], bank(g, A)[0:r, h, 0:r], col(gc, t, 4 * g + h, r), 0.0, ALU.subtract, ALU.max)
                        last.then_inc(ed[g], 1)
                    if t:
                        gate(t - 1)
                    for g in G2:
                        v.tensor_copy(T(g)[0:r, :, 0:r], m.ident[0:r, 0:r].unsqueeze(1).broadcast_to([r, 4, r])).then_inc(tcopy[g], 1)
                        dve.wait_ge(gram[g], t + 1)
                        dve.wait_ge(dd[g], t + 1)
                        for h in range(4):
                            last = v.scalar_tensor_tensor(nL[0:r, g, h, 0:r], bank(g, X)[0:r, h, 0:r], col(nbk, t, 4 * g + h, r),
                                                          Dd[0:r, g, h, 0:r], ALU.mult, ALU.mult)
                        last.then_inc(nl[g], 1)
                        dve.wait_ge(nl[g], t + 1)
                        dve.wait_ge(tcopy[g], 2 * t + 1)
                        v.copy_predicated(T(g)[0:r, :, 0:r], mask(0, r), nL[0:r, g, :, 0:r]).then_inc(t1[g], 1)
                        dve.wait_ge(attn[g], t + 1)
                        dve.wait_ge(dm[g], t + 1)
                        v.tensor_tensor(at[0:r, g, :, 0:r], bank(g, A)[0:r, :, 0:r], Dm[0:r, g, :, 0:r], ALU.mult).then_inc(atd[g], 1)
                    for l in range(1, LV[t] + 1):
                        for g in G2:
                            dve.wait_ge(ymm[g], base[t] + l)
                            if l > 1:
                                dve.wait_ge(uup[g], base[t] + l - 1)
                            v.copy_predicated(U(g)[0:r, :, 0:r], mask(l, r), bank(g, A)[0:r, :, 0:r]).then_inc(uup[g], 1)
                    for g in G2:
                        src = C if t < 4 else B
                        dve.wait_ge((ks if t < 4 else qs)[g], t + 1)
                        dve.wait_ge(vbd[g], t + 1)
                        for h in range(4):
                            last = v.scalar_tensor_tensor(W[0:r, g, h, :], bank(g, src)[0:r, h, :], col(nbe, t, 4 * g + h, r),
                                                          vb[0:r, g, h, :], ALU.mult, ALU.add)
                        last.then_inc(rd[g], 1)
                    for g in G2:
                        dve.wait_ge(av[g], t + 1)
                        dve.wait_ge(o1[g], t + 1)
                        v.tensor_tensor(on[0:r, g], on[0:r, g], bank(g, B)[0:r, :, :], ALU.add).then_inc(od[g], 1)
                        if t < 4:
                            dve.wait_ge(ds[g], t + 1)
                            if t:
                                dve.wait_ge(sd[g], t)
                            for h in range(4):
                                hh = 4 * g + h
                                last = v.scalar_tensor_tensor(S[:, hh, :], S[:, hh, :], egl[:, t, hh:hh + 1], bank(g, C)[:, h, :], ALU.mult, ALU.add)
                            last.then_inc(sd[g], 1)
                    if t == 4:
                        for i in range(8):
                            g = i % 2
                            dve.wait_ge(dsn, i + 1)
                            dve.wait_ge(smul, i + 1)
                            x = S0[:, i % 2].rearrange("p (a b) v -> p a (b v)", a=2)
                            v.tensor_tensor(x, x, psum[:, 4 * g + C:4 * g + C + 2, :], ALU.add).then_inc(sadd, 1)
                    for g in G2:
                        dve.wait_ge(sqd[g], t + 1)
                        v.tensor_reduce(ms[0:r, g, :], at[0:r, g], AX.X, ALU.add).then_inc(tcopy[g], 1)
                        dve.wait_ge(tcopy[g], 2 * t + 2)
                        v.tensor_tensor(ms[0:r, g, :], ms[0:r, g, :], cq2[0:r, t, 4 * g:4 * g + 4], ALU.mult).then_inc(v2[g], 1)
                gate(4)


def phase_merge(nc, m, ins, st, psum):
    with ExitStack() as ctx:
        sb = lambda name, shape, dt=F32: ctx.enter_context(nc.sbuf_tensor(name, shape, dt))
        sem = ctx.enter_context(semaphores(nc))
        mT = sb("mT", [128, KC, TOK])
        sg = sb("gate_sig", [128, 4, TOK])
        tb = sb("pb_gated", [128, 2, TOK])
        modp = sb("mod_prompt", [128, 3, D])
        modn = sb("mod_new", [64, 3, D])
        n2 = sb("norm2b", [128, D])
        h2 = sb("h2", [128, 2, D])
        xs = sb("x2_step", [128, 2, GW])
        ss, rstd = sb("x2_ss", [128, NT]), sb("x2_rstd", [128, NT])
        wr = sb("w_router", [128, KC, 36])
        lT = sb("logitsT", [36, TOK])
        xld, mld, rld = sem("x2_loaded"), sem("mod_loaded"), sem("router_loaded")
        gmm, gev, mev, tbd, init = sem("merge_mm"), sem("gate_ev"), sem("m_ev"), sem("pb_gated_done"), sem("m_init")
        omm, oev, x2d, sc2 = sem("o_mm"), sem("o_ev"), sem("x2_done"), sem("sc2_done")
        xsq, rsd, hsc, h2d, h2tr, h2ev, h2st = (sem(n) for n in ("x2_sq", "x2_rs", "h2_scaled", "h2_done", "h2_tr", "h2T_done", "h2_stored0"))
        h2st = [h2st, sem("h2_stored1")]
        lmm, lev, ltr, ld = sem("logit_mm"), sem("logit_ev"), sem("logit_tr"), sem("logit_done")
        first = st.at["ga0"]
        mod = lambda t: modp if t < 4 else modn
        with nc.Block() as block:
            @block.sync
            def _(sp):
                for i in range(8):
                    st.load(sp, first + 2 + i, (gmm, 4 * i + 4))
                for t in range(NT):
                    sp.wait_ge(h2d, t + 1)
                    sp.dma_start(m.h2_dram[tile_cols(t), :], h2[0:ROWS[t], t % 2, :]).then_inc(h2st[t % 2], 16)
                sp.wait_ge(h2st[0], 48)
                sp.wait_ge(h2st[1], 32)

            @block.gpsimd
            def _(pool):
                p = nc.gpsimd
                p.memset(ss[:, :], 1.0).then_inc(init, 1)
                p.memset(m.logits[:, :, :], 0.0).then_inc(init, 1)
                n = 0
                for j in range(2):
                    for t in range(NT):
                        r = ROWS[t]
                        pool.wait_ge(oev, NT * j + t + 1)
                        pool.wait_ge(xld, 80)
                        x = m.x2[0:r, t, GW * j:GW * j + GW]
                        p.tensor_tensor(x, x, xs[0:r, (NT * j + t) % 2, :], ALU.add).then_inc(x2d, 1)
                for t in range(NT):
                    r = ROWS[t]
                    pool.wait_ge(xsq, t + 1)
                    q = rstd[:, t:t + 1]
                    p.tensor_scalar(q, ss[:, t:t + 1], 1.0 / D, EPS, ALU.mult, ALU.add).then_inc(rsd, 1)
                    pool.wait_ge(rsd, 2 * t + 1)
                    p.tensor_tensor(q, q, m.half[:, 0:1], ALU.pow).then_inc(rsd, 1)
                    pool.wait_ge(hsc, t + 1)
                    p.tensor_tensor(h2[0:r, t % 2, :], h2[0:r, t % 2, :], mod(t)[0:r, 1, :], ALU.add).then_inc(h2d, 1)

            @block.scalar
            def _(act):
                a = nc.scalar
                for t in range(4):
                    act.dma_start(m.x2[:, t, :], ins["x_prompt"][0, tile_cols(t), :]).then_inc(xld, 16)
                act.dma_start(m.x2[0:64, 4, :], ins["x_sample"].rearrange("b s d -> (b s) d")).then_inc(xld, 16)
                act.dma_start(modp[:, :, :], m.mod_dram[0, 2 * D:5 * D].partition_broadcast(128)).then_inc(mld, 16)
                for b in range(NB):
                    act.dma_start(modn[NS * b:NS * b + NS], m.mod_dram[1 + b, 2 * D:5 * D].partition_broadcast(NS)).then_inc(mld, 16)
                act.dma_start(n2[:, :], ins["norm2"][0].partition_broadcast(128)).then_inc(mld, 16)
                act.dma_start(wr[:, :, 0:NG], ins["w_rg"][0].rearrange("(c p) n -> p c n", p=128)).then_inc(rld, 16)
                act.dma_start(wr[:, :, NG:36], ins["w_re"][0].rearrange("(c p) n -> p c n", p=128)).then_inc(rld, 16)
                act.dma_start(m.rbias[:, 0:NG], ins["b_rg"][0].partition_broadcast(128)).then_inc(rld, 16)
                act.dma_start(m.rbias[:, NG:36], ins["b_re"][0].partition_broadcast(128)).then_inc(rld, 16)
                for n in range(32):
                    q, gate = n // 4, (n // 4) % 2 == 0
                    if not gate:
                        continue
                    act.wait_ge(gmm, n + 1)
                    if n >= 8:
                        act.wait_ge(mev, 4 * (q // 2))
                    for hf in range(2):
                        last = a.activation(sg[:, n % 4, HALF * hf:HALF * hf + HALF], psum[:, 2 * (n % 4) + hf, 0:HALF], ACT.Sigmoid)
                    last.then_inc(gev, 1)
                act.wait_ge(init, 2)
                for t in range(NT):
                    act.wait_ge(x2d, NT + t + 1)
                    if t:
                        act.wait_ge(xsq, t)
                    a.activation(sg[0:ROWS[t], 0:2, 0:512], m.x2[0:ROWS[t], t, :].rearrange("p (a b) -> p a b", a=2), ACT.Square,
                                 accum_out=ss[0:ROWS[t], t:t + 1]).then_inc(xsq, 1)
                for t in range(NT):
                    r = ROWS[t]
                    act.wait_ge(h2tr, t + 1)
                    b = 4 + 2 * (t % 2)
                    a.copy(m.hT[:, :, tile_cols(t)].rearrange("p (a c) t -> p a c t", a=2),
                           psum[:, b:b + 2, :].rearrange("p a (c t) -> p a c t", t=128)[:, :, :, 0:r]).then_inc(h2ev, 1)
                act.wait_ge(lmm, 1)
                for hf in range(2):
                    last = a.copy(lT[:, HALF * hf:HALF * hf + HALF], psum[0:36, hf, 0:HALF])
                last.then_inc(lev, 1)

            @block.tensor
            def _(pe):
                te = nc.tensor
                for n in range(32):
                    q = n // 4
                    if n % 4 == 0:
                        w = st.wait(pe, first + q)
                    if n >= 4:
                        if (q - 1) % 2 == 0:
                            pe.wait_ge(gev, 4 * ((q - 1) // 2) + n % 4 + 1)
                        else:
                            pe.wait_ge(mev, 4 * ((q - 1) // 2) + n % 4 + 1)
                    x = m.hT if q % 2 == 0 else (m.aT if q < 4 else m.zzT)
                    project(nc, psum, 2 * (n % 4), w, n % 4, x).then_inc(gmm, 1)
                pe.wait_ge(mev, 16)
                pe.wait_ge(tbd, 8)
                for j in range(2):
                    w = st.wait(pe, first + 8 + j)
                    for t in range(NT):
                        i = NT * j + t
                        if i >= 4:
                            pe.wait_ge(oev, i - 3)
                        for c in range(KC):
                            last = te.matmul(psum[0:ROWS[t], i % 4, :], mT[:, c, tile_cols(t)], w[:, c, :], start=c == 0, stop=c == KC - 1)
                        last.then_inc(omm, 1)
                for t in range(NT):
                    r = ROWS[t]
                    pe.wait_ge(h2d, t + 1)
                    if t >= 2:
                        pe.wait_ge(h2ev, t - 1)
                    for c in range(KC):
                        last = te.transpose(psum[:, 4 + 2 * (t % 2) + c // 4, 128 * (c % 4):128 * (c % 4) + r],
                                            h2[0:r, t % 2, 128 * c:128 * c + 128], m.ident[0:r, 0:r])
                    last.then_inc(h2tr, 1)
                pe.wait_ge(h2ev, NT)
                pe.wait_ge(rld, 64)
                pe.wait_ge(oev, 10)
                for hf in range(2):
                    for c in range(KC):
                        last = te.matmul(psum[0:36, hf, 0:HALF], wr[:, c, :], m.hT[:, c, HALF * hf:HALF * hf + HALF], start=c == 0, stop=c == KC - 1)
                last.then_inc(lmm, 1)
                pe.wait_ge(lev, 1)
                for t in range(NT):
                    last = te.transpose(psum[0:ROWS[t], 2, 36 * t:36 * t + 36], lT[:, tile_cols(t)], m.ident[0:36, 0:36])
                last.then_inc(ltr, 1)

            @block.vector
            def _(dve):
                v = nc.vector
                k = 0
                for n in range(32):
                    q = n // 4
                    if q % 2 == 0:
                        continue
                    c = 4 * ((q // 2) % 2) + n % 4
                    dve.wait_ge(gmm, n + 1)
                    dve.wait_ge(gev, 4 * (q // 2) + n % 4 + 1)
                    b = 2 * (n % 4)
                    s3 = sg[:, n % 4, :].rearrange("p (a t) -> p a t", a=2)
                    out = mT[:, c, :] if q < 4 else tb[:, n % 2, :]
                    v.tensor_tensor(out.rearrange("p (a t) -> p a t", a=2), psum[:, b:b + 2, 0:HALF], s3, ALU.mult).then_inc(mev, 1)
                    if q >= 4:
                        dve.wait_ge(mev, k + 1)
                        v.tensor_tensor(mT[:, c, :], mT[:, c, :], tb[:, n % 2, :], ALU.add).then_inc(tbd, 1)
                    k += 1
                dve.wait_ge(mld, 16 * (NB + 2))
                v.scalar_tensor_tensor(modp[:, 2, :], modp[:, 2, :], 1.0, n2[:, :], ALU.add, ALU.mult)
                v.scalar_tensor_tensor(modn[:, 2, :], modn[:, 2, :], 1.0, n2[0:64, :], ALU.add, ALU.mult).then_inc(sc2, 1)
                for j in range(2):
                    for t in range(NT):
                        i = NT * j + t
                        r = ROWS[t]
                        dve.wait_ge(omm, i + 1)
                        if i >= 2:
                            dve.wait_ge(x2d, i - 1)
                        v.tensor_tensor(xs[0:r, i % 2, :], psum[0:r, i % 4, :], mod(t)[0:r, 0, GW * j:GW * j + GW], ALU.mult).then_inc(oev, 1)
                dve.wait_ge(sc2, 1)
                for t in range(NT):
                    r = ROWS[t]
                    dve.wait_ge(rsd, 2 * t + 2)
                    if t >= 2:
                        dve.wait_ge(h2tr, t - 1)
                        dve.wait_ge(h2st[t % 2], 16 * (t // 2))
                    v.scalar_tensor_tensor(h2[0:r, t % 2, :], m.x2[0:r, t, :], rstd[0:r, t:t + 1], mod(t)[0:r, 2, :], ALU.mult, ALU.mult).then_inc(hsc, 1)
                dve.wait_ge(ltr, 1)
                dve.wait_ge(init, 2)
                v.tensor_tensor(m.logits[:, 0:4, :], psum[:, 2, 0:144].rearrange("p (t r) -> p t r", t=4),
                                m.rbias[:, :].unsqueeze(1).broadcast_to([128, 4, 36]), ALU.add)
                v.tensor_tensor(m.logits[0:64, 4, :], psum[0:64, 2, 144:180], m.rbias[0:64, :], ALU.add).then_inc(ld, 1)


NBLK = 40
BIG = 1e30


def phase_route(nc, m, ins, psum):
    with ExitStack() as ctx:
        sb = lambda name, shape, dt=F32: ctx.enter_context(nc.sbuf_tensor(name, shape, dt))
        sem = ctx.enter_context(semaphores(nc))
        iota_i = sb("iota_i", [128, 128], I32)
        iota = sb("iota", [128, 128])
        desc = sb("desc", [128, 32])
        pair_i = sb("pair_i", [128, NT, 2], I32)
        pair1 = sb("pair1", [128, NT, 2])
        strict = sb("strict", [128, 128])
        gmax, gsum, gx = sb("gmax", [128, NT]), sb("gsum", [128, NT]), sb("gx", [128, NT, NG])
        gone = sb("gone", [128, NT, NG])
        em = sb("em", [128, NT, NE])
        sc = sb("score", [128, NT, NE])
        mx = sb("mx", [128, NT])
        mv = sb("mv", [128, 2, NT])
        one = sb("one", [128, 2, NT, NE])
        both = sb("both", [128, NT, NE])
        rank = sb("rank", [128, NT, NE])
        cnt = sb("cnt", [128, NE])
        nov, incl, excl = sb("nov", [128, NE]), sb("incl", [128, NE]), sb("excl", [128, NE])
        onesr = sb("ones_row", [128, NE])
        pr = sb("prod", [128, NT, NE])
        r_, e_, o_, q_ = (sb(n, [128, 2, NT]) for n in ("r_", "e_", "o_", "q_"))
        t_ = sb("t_", [128, 2, NT])
        slot, blk = sb("slot", [128, 2, NT]), sb("blk", [128, 2, NT])
        osl, obl = sb("onehot_slot", [128, 2, NT, 128]), sb("onehot_blk", [128, 2, NT, NBLK])
        tab, em0 = sb("tab", [128, NBLK]), sb("tab_empty", [128, NBLK])
        ovc = sb("ovc", [128, 8, NE])
        ovf = sb("ovf", [128, 9])
        ps, vs, pc, pt, ax, tp, ready = (sem(n) for n in ("r_pool", "r_dve", "r_count", "r_tab", "r_act", "r_idx", "r_ready"))
        with nc.Block() as block:
            @block.gpsimd
            def _(pool):
                p = nc.gpsimd
                n = [0]

                def step(i):
                    n[0] += 1
                    i.then_inc(ps, 1)
                    pool.wait_ge(ps, n[0])
                step(p.iota(iota_i[:, :], pattern=[[1, 128]], base=0, channel_multiplier=0))
                step(p.tensor_copy(iota[:, :], iota_i[:, :]))
                step(p.tensor_scalar(desc[:, :], iota[:, 0:32], -1.0, 32.0, ALU.mult, ALU.add))
                step(p.iota(pair_i[:, :, :], pattern=[[256, NT], [1, 2]], base=1, channel_multiplier=2))
                step(p.tensor_copy(pair1[:, :, :], pair_i[:, :, :]))
                step(p.memset(strict[:, :], 1.0))
                step(p.affine_select(out=strict[:, :], in_=strict[:, :], compare_op=ALU.is_gt, fill=0.0, base=0,
                                     pattern=[[1, 128]], channel_multiplier=-1))
                p.memset(onesr[:, :], 1.0).then_inc(ps, 1)

            @block.sync
            def _(sp):
                for u in range(2):
                    load_gate_up(sp, m, ins, u, u)
                    load_down(sp, m, ins, u, u)
                sp.dma_start(m.g2p[:, :], m.mod_dram[0, 5 * D:].partition_broadcast(128)).then_inc(m.g2_loaded, 16)
                for b in range(NB):
                    sp.dma_start(m.g2n[NS * b:NS * b + NS], m.mod_dram[1 + b, 5 * D:].partition_broadcast(NS)).then_inc(m.g2_loaded, 16)
                sp.dma_start(m.fnb[:, :], ins["final_norm"].partition_broadcast(128)).then_inc(m.g2_loaded, 16)

            @block.scalar
            def _(act):
                a = nc.scalar
                act.wait_ge(vs, 2)
                a.activation(gx[:, :, :], gx[:, :, :], ACT.Exp).then_inc(ax, 1)
                act.wait_ge(ready, 1)
                a.activation(m.w[:, :, 1], m.w[:, :, 1], ACT.Exp).then_inc(ax, 1)

            @block.tensor
            def _(pe):
                te = nc.tensor
                pe.wait_ge(ready, 2)
                pe.wait_ge(ps, 8)
                for t in range(NT):
                    r = ROWS[t]
                    for u in range(t):
                        te.matmul(psum[0:r, 0, 32 * t:32 * t + 32], m.blk[0][:, 0:r], both[:, u, :], start=u == 0, stop=False)
                    te.matmul(psum[0:r, 0, 32 * t:32 * t + 32], strict[0:r, 0:r], both[0:r, t, :], start=t == 0, stop=True)
                for t in range(NT):
                    r = ROWS[t]
                    last = te.matmul(psum[:, 1, 0:32], m.blk[0][0:r, :], both[0:r, t, :], start=t == 0, stop=t == NT - 1)
                last.then_inc(pc, 1)
                pe.wait_ge(ready, 3)
                for i, (t, k) in enumerate((t, k) for t in range(NT) for k in range(2)):
                    r = ROWS[t]
                    last = te.matmul(psum[:, 2, 0:NBLK], osl[0:r, k, t, :], obl[0:r, k, t, :], start=i == 0, stop=i == 9)
                last.then_inc(pt, 1)

            @block.vector
            def _(dve):
                v = nc.vector
                n = [0]

                def step(i):
                    n[0] += 1
                    i.then_inc(vs, 1)
                    dve.wait_ge(vs, n[0])
                glog = m.logits[:, :, 0:NG]
                elog = m.logits[:, :, NG:36].rearrange("p t (g e) -> p t g e", g=NG)
                bc = lambda x, k: x.unsqueeze(2).broadcast_to([128, NT, k])
                tt = lambda out, a, b, op: step(v.tensor_tensor(out, a, b, op))
                step(v.tensor_reduce(gmax[:, :], glog, AX.X, ALU.max))
                tt(gx[:, :, :], glog, bc(gmax[:, :], NG), ALU.subtract)
                tt(gone[:, :, :], glog, bc(gmax[:, :], NG), ALU.is_equal)
                dve.wait_ge(ps, 8)

                def first_of(out, k):
                    tt(out, out, desc[:, 0:k].unsqueeze(1).broadcast_to([128, NT, k]), ALU.mult)
                    step(v.tensor_reduce(mx[:, :], out, AX.X, ALU.max))
                    tt(out, out, bc(mx[:, :], k), ALU.is_equal)
                first_of(gone[:, :, :], NG)
                e4 = em[:, :, :].rearrange("p t (g e) -> p t g e", g=NG)
                g4 = gone[:, :, :].unsqueeze(3).broadcast_to([128, NT, NG, 8])
                s4 = sc[:, :, :].rearrange("p t (g e) -> p t g e", g=NG)
                for t in range(NT):
                    v.tensor_tensor(e4[:, t], elog[:, t], g4[:, t], ALU.mult)
                    last = v.tensor_scalar(s4[:, t], g4[:, t], BIG, -BIG, ALU.mult, ALU.add)
                step(last)
                tt(em[:, :, :], em[:, :, :], sc[:, :, :], ALU.add)
                for k in range(2):
                    step(v.tensor_reduce(mv[:, k, :], em[:, :, :], AX.X, ALU.max))
                    tt(one[:, k], em[:, :, :], bc(mv[:, k, :], NE), ALU.is_equal)
                    first_of(one[:, k], NE)
                    if k == 0:
                        step(v.scalar_tensor_tensor(em[:, :, :], one[:, 0], -1e38, em[:, :, :], ALU.mult, ALU.add))
                v.tensor_tensor(m.w[:, :, 1], mv[:, 1, :], mv[:, 0, :], ALU.subtract).then_inc(ready, 1)
                v.tensor_tensor(both[:, :, :], one[:, 0], one[:, 1], ALU.add).then_inc(ready, 1)
                dve.wait_ge(ax, 2)
                step(v.tensor_reduce(gsum[:, :], gx[:, :, :], AX.X, ALU.add))
                step(v.tensor_scalar(mx[:, :], m.w[:, :, 1], 1.0, None, ALU.add))
                tt(mx[:, :], mx[:, :], gsum[:, :], ALU.mult)
                step(v.reciprocal(m.w[:, :, 0], mx[:, :]))
                tt(m.w[:, :, 1], m.w[:, :, 1], m.w[:, :, 0], ALU.mult)
                dve.wait_ge(pc, 1)
                step(v.memset(rank[:, :, :], 0.0))
                v.tensor_copy(rank[:, 0:4, :].rearrange("p t e -> p (t e)"), psum[:, 0, 0:128])
                v.tensor_copy(rank[0:64, 4, :], psum[0:64, 0, 128:160])
                step(v.tensor_copy(cnt[:, :], psum[:, 1, 0:32]))

                def steps_of(out, x, tmp, lo):
                    step(v.tensor_scalar(out, x, float(lo), None, ALU.is_ge))
                    for k in range(1, 4):
                        step(v.scalar_tensor_tensor(out, x, float(lo + 128 * k), out, ALU.is_ge, ALU.add))
                steps_of(nov[:, :], cnt[:, :], None, 129)
                step(v.tensor_tensor_scan(incl[:, :], onesr[:, :], nov[:, :], 0.0, ALU.mult, ALU.add))
                tt(excl[:, :], incl[:, :], nov[:, :], ALU.subtract)
                for k in range(2):
                    for out, x in ((r_, rank[:, :, :]), (e_, iota[:, 0:32].unsqueeze(1).broadcast_to([128, NT, NE])),
                                   (o_, excl[:, :].unsqueeze(1).broadcast_to([128, NT, NE]))):
                        tt(pr[:, :, :], one[:, k], x, ALU.mult)
                        step(v.tensor_reduce(out[:, k, :], pr[:, :, :], AX.X, ALU.add))
                flat = lambda x: x[:, :, :].rearrange("p k t -> p (k t)")
                steps_of(flat(q_), flat(r_), None, 128)
                step(v.scalar_tensor_tensor(flat(slot), flat(q_), -128.0, flat(r_), ALU.mult, ALU.add))
                tt(flat(t_), flat(o_), flat(q_), ALU.add)
                tt(flat(t_), flat(t_), flat(e_), ALU.subtract)
                step(v.tensor_scalar(flat(t_), flat(t_), float(NE - 1), None, ALU.add))
                step(v.tensor_scalar(flat(q_), flat(q_), 1.0, None, ALU.min))
                tt(flat(t_), flat(t_), flat(q_), ALU.mult)
                tt(flat(blk), flat(t_), flat(e_), ALU.add)
                for t in range(NT):
                    for k in range(2):
                        v.tensor_scalar(osl[:, k, t, :], iota[:, :], slot[:, k, t:t + 1], None, ALU.is_equal)
                        last = v.tensor_scalar(obl[:, k, t, :], iota[:, 0:NBLK], blk[:, k, t:t + 1], pair1[:, t, k:k + 1], ALU.is_equal, ALU.mult)
                last.then_inc(ready, 1)
                for b in range(8):
                    last = v.tensor_scalar(ovc[:, b, :], incl[:, :], float(b), None, ALU.is_le)
                step(last)
                step(v.tensor_reduce(ovf[:, 0:8], ovc[:, :, :], AX.X, ALU.add))
                step(v.tensor_scalar(ovf[:, 0:8], ovf[:, 0:8], float(NE - 1), None, ALU.min))
                step(v.tensor_copy(ovf[:, 8:9], incl[:, NE - 1:NE]))
                step(v.tensor_copy(m.over[:, :], ovf[:, :]))
                dve.wait_ge(pt, 1)
                step(v.tensor_copy(tab[:, :], psum[:, 2, 0:NBLK]))
                step(v.tensor_scalar(em0[:, :], tab[:, :], 0.0, 65536.0, ALU.is_equal, ALU.mult))
                step(v.scalar_tensor_tensor(tab[:, :], em0[:, :], -1.0, tab[:, :], ALU.add, ALU.add))
                step(v.memset(m.pairs[:, :], 65536))
                step(v.tensor_copy(m.pairs[:, 0:NBLK], tab[:, :]))
                step(v.tensor_scalar(m.toks[:, :], m.pairs[:, :], 1, None, ALU.logical_shift_right))


def load_gate_up(sp, m, ins, e, u):
    for k, name in enumerate(("w_e_gate", "w_e_up")):
        w = ins[name][0].rearrange("g e (p c) f -> (g e) p c f", p=128)
        sp.dma_start(m.gu[:, u, k], w[e]).then_inc(m.gu_loaded[u], 16)


def load_down(sp, m, ins, e, u):
    w = ins["w_e_down"][0].rearrange("g e (p c) d -> (g e) p c d", p=128)
    sp.dma_start(m.wd[:, u], w[e]).then_inc(m.wd_loaded[u], 16)


def phase_moe(nc, m, ins, psum):
    with ExitStack() as ctx:
        sb = lambda name, shape, dt=F32: ctx.enter_context(nc.sbuf_tensor(name, shape, dt))
        sem = ctx.enter_context(semaphores(nc))
        gu, wd, gld, dld = m.gu, m.wd, m.gu_loaded, m.wd_loaded
        xg, xT = sb("x_gathered", [128, 2, D]), sb("xT", [128, 2, KC, 128])
        sg, ac, aT = sb("silu_gate", [128, 2, DE]), sb("act", [128, 2, DE]), sb("actT", [128, 2, 2, 128])
        yo = sb("y_block", [128, 2, D])
        ti, pi = sb("tok_idx", [128, 2], U32), sb("pair_idx", [128, 2], U32)
        gth, sct = ([sem(f"{n}{u}") for u in range(2)] for n in ("gathered", "scattered"))
        start, issued, idx, pidx, xtr, xev, gmm, sgd, acd, atr, aev, dmm, yev = (sem(n) for n in (
            "moe_start", "moe_issued", "idx_copied", "pair_idx_copied", "moe_xtr", "moe_xev", "moe_gu", "moe_silu", "moe_act", "moe_atr", "moe_aev", "moe_down", "moe_yev"))
        OVER = [(0, NE // 2), (NE // 2, NBLK // 2)]

        def both_ranges(eng, body, after=None, first=0):
            with eng.Fori(first, OVER[0][1]) as i:
                body(2 * i, False)
            if after:
                after(0)
            n = eng.value_load(m.over[0:1, 8:9], min_val=0, max_val=8)
            with eng.If(n > 0):
                with eng.Fori(*OVER[1]) as i:
                    body(2 * i, True)
                if after:
                    after(1)
                eng.nop()
            with eng.Else():
                eng.nop()

        FROM = 2
        done = lambda b: b + 1 + FROM
        back2 = lambda b: b - 1 + FROM
        gu_in = lambda b0: 16 * b0 + 32
        one_in = lambda b0: 8 * b0 + 16
        with nc.Block() as block:
            @block.sync
            def _(sp):
                def body(b0, over):
                    expert = [b0, b0 + 1]
                    if over:
                        expert = [sp.value_load(m.over[0:1, bass.ds(b0 + (u - NE), 1)], min_val=0, max_val=NE - 1) for u in range(2)]
                    for u in range(2):
                        sp.wait_ge(gmm, back2(b0 + u))
                        load_gate_up(sp, m, ins, expert[u], u)
                    for u in range(2):
                        sp.wait_ge(dmm, back2(b0 + u))
                        load_down(sp, m, ins, expert[u], u)
                both_ranges(sp, body, first=1)

            @block.gpsimd
            def _(pool):
                p = nc.gpsimd
                p.memset(xg[:, :, :], 0.0).then_inc(start, 1)
                pool.wait_ge(start, 1)
                for u in range(2):
                    p.dma_start(pi[:, u:u + 1], m.pairs[:, u:u + 1]).then_inc(sct[u], 16)
                last_tok, last_pair = p.to_reg(TOK - 1), p.to_reg(2 * TOK - 1)

                def gather(b, u):
                    pool.wait_ge(idx, done(b))
                    pool.wait_ge(xtr, back2(b))
                    p.sem_inc(issued, 1)
                    p.indirect_dma_start(out=xg[:, u, :], out_offset=None, in_=m.h2_dram[:, :],
                                         in_offset=bass.IndirectOffsetOnAxis(ap=ti[:, u:u + 1], axis=0),
                                         bounds_check=last_tok, oob_is_err=False).then_inc(gth[u], 16)

                def scatter(b, u):
                    pool.wait_ge(yev, done(b))
                    pool.wait_ge(pidx, done(b))
                    p.sem_inc(issued, 1)
                    p.indirect_dma_start(out=m.y_dram[:, :], out_offset=bass.IndirectOffsetOnAxis(ap=pi[:, u:u + 1], axis=0),
                                         in_=yo[:, u, :], in_offset=None,
                                         bounds_check=last_pair, oob_is_err=False).then_inc(sct[u], 16)

                for u in range(2):
                    gather(u, u)

                def body(b0, over):
                    for u in range(2):
                        gather(b0 + (2 + u), u)
                    for u in range(2):
                        scatter(b0 + u, u)

                def after(k):
                    for u in range(2):
                        pool.wait_ge(gth[u], 16 * (OVER[k][1] + 1))
                        pool.wait_ge(sct[u], 16 * (OVER[k][1] + 1))
                both_ranges(pool, body, after)

            @block.scalar
            def _(act):
                a = nc.scalar
                a.sem_inc(sgd, FROM)
                a.sem_inc(yev, FROM)

                def body(b0, over):
                    for u in range(2):
                        b = b0 + u
                        act.wait_ge(gmm, done(b))
                        act.wait_ge(acd, back2(b))
                        a.activation(sg[:, u, :], psum[:, u, 0:DE], ACT.Silu).then_inc(sgd, 1)
                    for u in range(2):
                        b = b0 + u
                        act.wait_ge(dmm, done(b))
                        act.wait_ge(sct[u], one_in(b0))
                        a.copy(yo[:, u, :].rearrange("p (a d) -> p a d", a=2), psum[:, 4 + 2 * u:6 + 2 * u, :]).then_inc(yev, 1)
                both_ranges(act, body)

            @block.tensor
            def _(pe):
                te = nc.tensor
                for s in (xtr, gmm, atr, dmm):
                    te.sem_inc(s, FROM)

                def x_transposes(b0, n):
                    u = n % 2
                    pe.wait_ge(gth[u], one_in(b0 + 2 * (n // 2)))
                    for c in range(KC):
                        last = te.transpose(psum[:, 2 + c // 4, 128 * (c % 4):128 * (c % 4) + 128], xg[:, u, c::KC], m.ident[:, :])
                    last.then_inc(xtr, 1)

                x_transposes(0, 0)

                def gate_up(b0, u):
                    pe.wait_ge(gld[u], gu_in(b0))
                    pe.wait_ge(xev, done(b0 + u))
                    pe.wait_ge(acd, back2(b0 + u))
                    for c in range(KC):
                        last = te.matmul(psum[:, u, :], xT[:, u, c, :], gu[:, u, :, c, :], start=c == 0, stop=c == KC - 1)
                    last.then_inc(gmm, 1)

                def act_transposes(b0, u):
                    pe.wait_ge(acd, done(b0 + u))
                    if u == 0:
                        pe.wait_ge(yev, back2(b0 + 1))
                    for c in range(2):
                        last = te.transpose(psum[:, 6 + u, 128 * c:128 * c + 128], ac[:, u, c::2], m.ident[:, :])
                    last.then_inc(atr, 1)

                def down(b0, u):
                    pe.wait_ge(aev, b0 + 2 + FROM)
                    pe.wait_ge(dld[u], one_in(b0))
                    pe.wait_ge(yev, back2(b0 + u))
                    for hf in range(2):
                        for c in range(2):
                            last = te.matmul(psum[:, 4 + 2 * u + hf, :], aT[:, u, c, :], wd[:, u, c, 512 * hf:512 * hf + 512],
                                             start=c == 0, stop=c == 1)
                    last.then_inc(dmm, 1)

                def body(b0, over):
                    pe.wait_ge(xev, done(b0))
                    x_transposes(b0, 1)
                    gate_up(b0, 0)
                    gate_up(b0, 1)
                    act_transposes(b0, 0)
                    x_transposes(b0, 2)
                    act_transposes(b0, 1)
                    down(b0, 0)
                    down(b0, 1)
                both_ranges(pe, body)

            @block.vector
            def _(dve):
                v = nc.vector
                for s in (idx, pidx, xev, acd, aev):
                    v.sem_inc(s, FROM)

                def x_evacuate(b, u):
                    dve.wait_ge(xtr, done(b))
                    v.tensor_copy(xT[:, u].rearrange("p (a c) s -> p a (c s)", a=2), psum[:, 2:4, :]).then_inc(xev, 1)

                for u in range(2):
                    v.tensor_copy(ti[:, u:u + 1], m.toks[:, u:u + 1]).then_inc(idx, 1)
                x_evacuate(0, 0)

                def product(b, u):
                    dve.wait_ge(sgd, done(b))
                    v.tensor_tensor(ac[:, u, :], sg[:, u, :], psum[:, u, DE:2 * DE], ALU.mult).then_inc(acd, 1)

                def act_evacuate(b, u):
                    dve.wait_ge(atr, done(b))
                    v.tensor_copy(aT[:, u].rearrange("p c s -> p (c s)"), psum[:, 6 + u, 0:256]).then_inc(aev, 1)

                def body(b0, over):
                    for u in range(2):
                        dve.wait_ge(gth[u], one_in(b0))
                        v.tensor_copy(ti[:, u:u + 1], m.toks[:, bass.ds(b0 + (u + 2), 1)]).then_inc(idx, 1)
                    x_evacuate(b0 + 1, 1)
                    product(b0, 0)
                    act_evacuate(b0, 0)
                    product(b0 + 1, 1)
                    x_evacuate(b0 + 2, 0)
                    act_evacuate(b0 + 1, 1)
                    for u in range(2):
                        dve.wait_ge(sct[u], one_in(b0))
                        v.tensor_copy(pi[:, u:u + 1], m.pairs[:, bass.ds(b0 + u, 1)]).then_inc(pidx, 1)
                both_ranges(dve, body)


def phase_final(nc, m, ins, outs, psum):
    with ExitStack() as ctx:
        sb = lambda name, shape, dt=F32: ctx.enter_context(nc.sbuf_tensor(name, shape, dt))
        sem = ctx.enter_context(semaphores(nc))
        y = sb("y_pairs", [128, NT, 2, D])
        gp, gn, fn = m.g2p, m.g2n, m.fnb
        sq = sb("fin_sq", [128, D])
        ss, rs = sb("fin_ss", [128, NT]), sb("fin_rs", [128, NT])
        yl = [sem(f"y_loaded{t}") for t in range(NT)]
        init, ya, yb, yg, x3, fq, fr, xn, fo = (sem(n) for n in ("f_init", "y1_weighted", "y_summed", "y_gated", "x3_done", "f_sq", "f_rs", "x3_normed", "f_out"))
        y0 = lambda t: y[0:ROWS[t], t, 0, :]
        x = lambda t: m.x2[0:ROWS[t], t, :]
        with nc.Block() as block:
            @block.sync
            def _(sp):
                for t in range(NT):
                    r = ROWS[t]
                    sp.dma_start(y[0:r, t], m.y_dram[256 * t:256 * t + 2 * r, :].rearrange("(p k) d -> p k d", k=2)).then_inc(yl[t], 16)
                for t in range(NT):
                    sp.wait_ge(fo, t + 1)
                    out = outs["y_prompt"][0, tile_cols(t), :] if t < 4 else outs["y_sample"].rearrange("b s d -> (b s) d")
                    sp.dma_start(out, y0(t)).then_inc(m.y_stored, 16)
                sp.wait_ge(m.y_stored, 16 * NT)

            @block.gpsimd
            def _(pool):
                p = nc.gpsimd
                p.memset(ss[:, :], 1.0).then_inc(init, 1)
                pool.wait_ge(m.g2_loaded, 16 * (NB + 2))

                def norm(t):
                    q = rs[:, t:t + 1]
                    pool.wait_ge(fq, t + 1)
                    p.tensor_scalar(q, ss[:, t:t + 1], 1.0 / D, EPS, ALU.mult, ALU.add).then_inc(fr, 1)
                    pool.wait_ge(fr, 2 * t + 1)
                    p.tensor_tensor(q, q, m.half[:, 0:1], ALU.pow).then_inc(fr, 1)

                for t in range(NT):
                    pool.wait_ge(yb, t + 1)
                    p.tensor_tensor(y0(t), y0(t), (gp if t < 4 else gn)[0:ROWS[t], :], ALU.mult).then_inc(yg, 1)
                    if t:
                        norm(t - 1)
                norm(NT - 1)

            @block.scalar
            def _(act):
                a = nc.scalar
                for t in range(NT):
                    act.wait_ge(yl[t], 16)
                    a.activation(y0(t), y0(t), ACT.Copy, scale=m.w[0:ROWS[t], t, 0:1]).then_inc(ya, 1)
                act.wait_ge(init, 1)
                for t in range(NT + 1):
                    if t < NT:
                        act.wait_ge(x3, t + 1)
                        if t:
                            act.wait_ge(fq, t)
                        a.activation(sq[0:ROWS[t], :], x(t), ACT.Square, accum_out=ss[0:ROWS[t], t:t + 1]).then_inc(fq, 1)
                    if t:
                        act.wait_ge(fr, 2 * t)
                        act.wait_ge(fq, t)
                        a.activation(x(t - 1), x(t - 1), ACT.Copy, scale=rs[0:ROWS[t - 1], t - 1:t]).then_inc(xn, 1)

            @block.vector
            def _(dve):
                v = nc.vector
                dve.wait_ge(m.g2_loaded, 16 * (NB + 2))
                for t in range(NT + 2):
                    if t < NT:
                        dve.wait_ge(ya, t + 1)
                        v.scalar_tensor_tensor(y0(t), y[0:ROWS[t], t, 1, :], m.w[0:ROWS[t], t, 1:2], y0(t), ALU.mult, ALU.add).then_inc(yb, 1)
                    if 1 <= t <= NT:
                        dve.wait_ge(yg, t)
                        v.tensor_tensor(x(t - 1), x(t - 1), y0(t - 1), ALU.add).then_inc(x3, 1)
                    if t >= 2:
                        dve.wait_ge(xn, t - 1)
                        v.tensor_tensor(y0(t - 2), x(t - 2), fn[0:ROWS[t - 2], :], ALU.mult).then_inc(fo, 1)


def program(nc, ins, outs, upto=99):
    ctx = ExitStack()
    with ctx:
        m = Mem()
        sb = lambda name, shape, dt=F32: ctx.enter_context(nc.sbuf_tensor(name, shape, dt))
        m.mod_dram = nc.dram_tensor("mod_scratch", (9, 6 * D), F32, kind="Internal").ap()
        m.h2_dram = nc.dram_tensor("h2_scratch", (TOK, D), F32, kind="Internal").ap()
        m.y_dram = nc.dram_tensor("pair_scratch", (2 * TOK, D), F32, kind="Internal").ap()
        kept = lambda name: ctx.enter_context(nc.semaphore(name))
        m.chunk_v_stored, m.conv_stored, m.y_stored = kept("chunk_v_stored"), kept("conv_stored"), kept("y_stored")
        m.delta0_stored, m.delta1_stored, m.delta_p_stored = kept("delta0_stored"), kept("delta1_stored"), kept("delta_p_stored")
        psum = ctx.enter_context(nc.psum_tensor("ps", [128, 8, 512], F32))
        st = Stream(nc, ctx, ins)
        constants(nc, ctx, m)
        m.convT = sb("convT", [128, 97])
        m.hT = sb("hT", [128, KC, TOK])
        phase_modulation(nc, m, ins, st, psum)
        if upto == 1:
            return dump(nc, outs["dbg"], m.hT[:, :, :].rearrange("p c t -> p (c t)"))
        m.aT = sb("aT", [128, KC, TOK])
        phase_gmlp(nc, m, ins, outs, st, psum)
        m.zzT = sb("zzT", [128, KC, TOK])
        if upto == 2:
            return dump(nc, outs["dbg"], m.aT[:, :, :].rearrange("p c t -> p (c t)"))
        m.ba = sb("ba", [128, NT, 16])
        m.ss = sb("ss_qk", [128, NT, 16])
        dctx = ctx.enter_context(ExitStack())
        m.qkvT = dctx.enter_context(nc.sbuf_tensor("qkvT", [128, NCH, TOK], F32))
        phase_qkv(nc, m, ins, outs, st, psum)
        if upto == 3:
            return dump(nc, outs["dbg"], m.qkvT[:, :, :].rearrange("p c t -> p (c t)"))
        phase_delta(nc, m, ins, outs, psum)
        dctx.close()
        if upto == 4:
            return dump(nc, outs["dbg"], m.zzT[:, :, :].rearrange("p c t -> p (c t)"))
        m.x2 = sb("x2", [128, NT, D])
        m.logits, m.rbias = sb("logits", [128, NT, 36]), sb("rbias", [128, 36])
        phase_merge(nc, m, ins, st, psum)
        if upto == 5:
            return dump(nc, outs["dbg"], m.x2[:, :, :].rearrange("p c t -> p (c t)"))
        m.w = sb("pair_weight", [128, NT, 2])
        m.over = sb("over", [128, 9], I32)
        m.pairs, m.toks = sb("pairs", [128, NBLK + 2], U32), sb("toks", [128, NBLK + 2], U32)
        m.gu_loaded, m.wd_loaded = ([kept(f"{n}{u}") for u in range(2)] for n in ("gu_loaded", "wd_loaded"))
        m.g2p, m.g2n, m.fnb = sb("g2_prompt", [128, D]), sb("g2_new", [64, D]), sb("final_norm_b", [128, D])
        m.g2_loaded = kept("g2_loaded")
        ectx = ctx.enter_context(ExitStack())
        m.gu = ectx.enter_context(nc.sbuf_tensor("w_gate_up", [128, 2, 2, KC, DE], F32))
        m.wd = ectx.enter_context(nc.sbuf_tensor("w_down", [128, 2, 2, D], F32))
        phase_route(nc, m, ins, psum)
        phase_moe(nc, m, ins, psum)
        ectx.close()
        phase_final(nc, m, ins, outs, psum)


def dump(nc, out, ap):
    with nc.semaphore("dump") as s, nc.Block() as block:
        @block.sync
        def _(sp):
            sp.dma_start(out, ap).then_inc(s, 16)
            sp.wait_ge(s, 16)


_OUTS = [("y_prompt", (1, SEQ, D)), ("y_sample", (NB, NS, D)), ("conv_prompt", (1, 1, HIST, 3 * D)),
         ("conv_sample", (1, NB, HIST, 3 * D)), ("delta_prompt", (1, 1, H, 128, 128)),
         ("delta_sample", (1, NB, H, 128, 128)), ("chunk_v_sample", (1, NB, NS, D))]


def kernel(**inputs):
    import concourse.bacc as bacc
    from concourse.bass_utils import run_bass_kernel_spmd

    nc = bacc.Bacc("TRN2", target_bir_lowering=False, num_devices=1)
    arrays = {name: np.ascontiguousarray(a) for name, a in inputs.items()}
    ins = {name: nc.dram_tensor(name, a.shape, mybir.dt.from_np(a.dtype), kind="ExternalInput").ap()
           for name, a in arrays.items()}
    outs = {name: nc.dram_tensor(name, shape, F32, kind="ExternalOutput").ap() for name, shape in _OUTS}
    program(nc, ins, outs)
    r = run_bass_kernel_spmd(nc, [arrays], core_ids=[0])
    return tuple(r.results[0][name] for name, _ in _OUTS)
```
